# Optimizing a Trainium2 kernel written in Bass

```python
import jax, jax.numpy as jnp
from jax import lax
import numpy as np

D_MODEL = 1024
BATCH = 1
SEQ = 256
DEPTH = 2

N_META = 16
ATTN_HEADS = 8
ATTN_KV_HEADS = 2
HEAD_DIM = 64
WINDOW = 128
BLOCK = 128
ATTN_WIDTH = ATTN_HEADS * HEAD_DIM
KV_WIDTH = ATTN_KV_HEADS * HEAD_DIM
SSM_HEAD_DIM = 64
SSM_HEADS = 24
SSM_D_INNER = SSM_HEADS * SSM_HEAD_DIM
SSM_GROUPS = 2
SSM_STATE = 128
CONV_K = 4
CHUNK = 128
CONV_DIM = SSM_D_INNER + 2 * SSM_GROUPS * SSM_STATE
MIX_WIDTH = ATTN_WIDTH + SSM_D_INNER
IN_PROJ = ATTN_WIDTH + 2 * KV_WIDTH + SSM_D_INNER + CONV_DIM + SSM_HEADS
D_FF = 3584
N_EXPERTS = 8
TOP_K = 2
N_DENSE = (DEPTH + 1) // 2
N_MOE = DEPTH // 2
EPS = 1e-6

kernel_name = "hymba_ssd_swa_sink_moe_trunk"

def rmsnorm(x, g):
    xf = x.astype(jnp.float32)
    y = xf * lax.rsqrt(jnp.mean(xf * xf, axis=-1, keepdims=True) + EPS)
    return (y * g.astype(jnp.float32)).astype(x.dtype)

def causal_dwconv(u, w, b):
    rhs = jnp.transpose(w)[:, None, :].astype(u.dtype)
    y = lax.conv_general_dilated(u, rhs, window_strides=(1,), padding=[(CONV_K - 1, 0)],
                                 dimension_numbers=("NWC", "WIO", "NWC"),
                                 feature_group_count=u.shape[-1])
    return y + b.astype(u.dtype)

def ssd_scan(xs, dt, a, bm, cm):
    f32 = jnp.float32
    bsz, lp = xs.shape[:2]
    nc = lp // CHUNK
    hg = SSM_HEADS // SSM_GROUPS
    xdt = (xs.astype(f32) * dt[..., None]).reshape(bsz, nc, CHUNK, SSM_GROUPS, hg, SSM_HEAD_DIM)
    bc = bm.astype(f32).reshape(bsz, nc, CHUNK, SSM_GROUPS, SSM_STATE)
    cc = cm.astype(f32).reshape(bsz, nc, CHUNK, SSM_GROUPS, SSM_STATE)
    da = (dt * a).reshape(bsz, nc, CHUNK, SSM_GROUPS, hg).transpose(0, 1, 3, 4, 2)
    a_cs = jnp.cumsum(da, axis=-1)
    causal = jnp.tril(jnp.ones((CHUNK, CHUNK), dtype=bool))
    seg = a_cs[..., :, None] - a_cs[..., None, :]
    decay_in = jnp.exp(jnp.where(causal, seg, -jnp.inf))
    cb = jnp.einsum("bclgn,bcsgn->bcgls", cc, bc)
    w_intra = cb[:, :, :, None] * decay_in
    y_diag = jnp.einsum("bcghls,bcsghp->bclghp", w_intra, xdt)
    decay_st = jnp.exp(a_cs[..., -1:] - a_cs).transpose(0, 1, 4, 2, 3)[..., None]
    states = jnp.einsum("bcsgn,bcsghp->bcghpn", bc, xdt * decay_st)
    chunk_decay = jnp.exp(a_cs[..., -1])

    def step(h, inp):
        st, dec = inp
        return h * dec[..., None, None] + st, h

    h0 = jnp.zeros((bsz, SSM_GROUPS, hg, SSM_HEAD_DIM, SSM_STATE), f32)
    _, h_prev = lax.scan(step, h0, (states.transpose(1, 0, 2, 3, 4, 5),
                                    chunk_decay.transpose(1, 0, 2, 3)))
    h_prev = h_prev.transpose(1, 0, 2, 3, 4, 5)
    decay_out = jnp.exp(a_cs).transpose(0, 1, 4, 2, 3)[..., None]
    y_off = jnp.einsum("bclgn,bcghpn->bclghp", cc, h_prev) * decay_out
    return (y_diag + y_off).reshape(bsz, lp, SSM_HEADS, SSM_HEAD_DIM)

def swa_sink_attention(q, k, v, sinks):
    f32 = jnp.float32
    bsz, seqlen = q.shape[:2]
    pad = BLOCK - N_META
    rep = ATTN_HEADS // ATTN_KV_HEADS
    k_meta, v_meta = k[:, :N_META], v[:, :N_META]
    padw = ((0, 0), (pad, 0), (0, 0), (0, 0))
    lp = seqlen + pad
    nb = lp // BLOCK
    qb = jnp.pad(q, padw).reshape(bsz, nb, BLOCK, ATTN_KV_HEADS, rep, HEAD_DIM)
    kb = jnp.pad(k, padw).reshape(bsz, nb, BLOCK, ATTN_KV_HEADS, HEAD_DIM)
    vb = jnp.pad(v, padw).reshape(bsz, nb, BLOCK, ATTN_KV_HEADS, HEAD_DIM)

    def band(t):
        prev = jnp.pad(t[:, :-1], ((0, 0), (1, 0), (0, 0), (0, 0), (0, 0)))
        return jnp.concatenate([prev, t], axis=2)

    kband, vband = band(kb), band(vb)
    qpos = jnp.arange(nb)[:, None] * BLOCK + jnp.arange(BLOCK)[None, :] - pad
    kpos = jnp.arange(nb)[:, None] * BLOCK + jnp.arange(-BLOCK, BLOCK)[None, :] - pad
    band_mask = ((kpos[:, None, :] <= qpos[:, :, None])
                 & (qpos[:, :, None] - kpos[:, None, :] < WINDOW)
                 & (kpos[:, None, :] >= N_META))
    meta_mask = jnp.arange(N_META)[None, None, :] <= qpos[:, :, None]
    mask = jnp.concatenate([meta_mask, band_mask], axis=-1)
    scale = HEAD_DIM ** -0.5
    s_meta = jnp.einsum("bnqkrd,bmkd->bnkrqm", qb, k_meta)
    s_band = jnp.einsum("bnqkrd,bnskd->bnkrqs", qb, kband)
    s = jnp.concatenate([s_meta, s_band], axis=-1).astype(f32) * scale
    s = jnp.where(mask[None, :, None, None], s, -jnp.inf)
    sink = jnp.broadcast_to(sinks.astype(f32).reshape(ATTN_KV_HEADS, rep)[None, None, :, :, None, None],
                            s.shape[:-1] + (1,))
    p = jax.nn.softmax(jnp.concatenate([s, sink], axis=-1), axis=-1)[..., :-1].astype(v.dtype)
    o = (jnp.einsum("bnkrqm,bmkd->bnqkrd", p[..., :N_META], v_meta)
         + jnp.einsum("bnkrqs,bnskd->bnqkrd", p[..., N_META:], vband))
    return o.reshape(bsz, lp, ATTN_WIDTH)[:, pad:]

def hybrid_mixer(h, w_in, conv_w, conv_b, dt_bias, a_log, d_skip, ssm_norm, attn_norm, sinks, w_out):
    f32 = jnp.float32
    bsz, seqlen, _ = h.shape
    proj = h @ w_in
    cuts = np.cumsum([ATTN_WIDTH, KV_WIDTH, KV_WIDTH, SSM_D_INNER, CONV_DIM]).tolist()
    q, k, v, z, xbc, dt_raw = jnp.split(proj, cuts, axis=-1)
    q = q.reshape(bsz, seqlen, ATTN_HEADS, HEAD_DIM)
    k = k.reshape(bsz, seqlen, ATTN_KV_HEADS, HEAD_DIM)
    v = v.reshape(bsz, seqlen, ATTN_KV_HEADS, HEAD_DIM)
    y_attn = rmsnorm(swa_sink_attention(q, k, v, sinks), attn_norm)
    xbc = jax.nn.silu(causal_dwconv(xbc, conv_w, conv_b))
    xs, bm, cm = jnp.split(xbc, [SSM_D_INNER, SSM_D_INNER + SSM_GROUPS * SSM_STATE], axis=-1)
    xs = xs.reshape(bsz, seqlen, SSM_HEADS, SSM_HEAD_DIM)
    bm = bm.reshape(bsz, seqlen, SSM_GROUPS, SSM_STATE)
    cm = cm.reshape(bsz, seqlen, SSM_GROUPS, SSM_STATE)
    dt = jax.nn.softplus(dt_raw.astype(f32) + dt_bias.astype(f32))
    a = -jnp.exp(a_log.astype(f32))
    pad = CHUNK - N_META

    def padl(t):
        return jnp.pad(t, ((0, 0), (pad, 0)) + ((0, 0),) * (t.ndim - 2))

    y = ssd_scan(padl(xs), padl(dt), a, padl(bm), padl(cm))[:, pad:]
    y = y + xs.astype(f32) * d_skip.astype(f32)[:, None]
    y = y.reshape(bsz, seqlen, SSM_D_INNER) * jax.nn.silu(z.astype(f32))
    yg = y.reshape(bsz, seqlen, SSM_GROUPS, SSM_D_INNER // SSM_GROUPS)
    yg = yg * lax.rsqrt(jnp.mean(yg * yg, axis=-1, keepdims=True) + EPS)
    y_ssm = (yg.reshape(bsz, seqlen, SSM_D_INNER) * ssm_norm.astype(f32)).astype(h.dtype)
    return jnp.concatenate([y_attn, y_ssm], axis=-1) @ w_out

def swiglu(t, w1, w3, w2):
    return (jax.nn.silu(t @ w1) * (t @ w3)) @ w2

def moe_swiglu(u, router, w1, w3, w2):
    t = u.reshape(-1, D_MODEL)
    logits = (t @ router).astype(jnp.float32)
    top_v, top_i = lax.top_k(logits, TOP_K)
    gates = jax.nn.softmax(top_v, axis=-1)
    comb = jnp.einsum("nk,nke->ne", gates,
                      jax.nn.one_hot(top_i, N_EXPERTS, dtype=jnp.float32)).astype(u.dtype)
    out = jnp.zeros_like(t)
    for e in range(N_EXPERTS):
        out = out + comb[:, e:e + 1] * swiglu(t, w1[e], w3[e], w2[e])
    return out.reshape(u.shape)

def setup_inputs(seed: int = 0) -> dict:
    key = jax.random.key(seed)
    ks = jax.random.split(key, 24)
    f = jnp.float32

    def nrm(k, shape, scale):
        return jax.random.normal(k, shape, f) * scale

    dt0 = jnp.exp(jax.random.uniform(ks[6], (DEPTH, SSM_HEADS), f)
                  * (jnp.log(0.1) - jnp.log(0.001)) + jnp.log(0.001))
    return {
        "x": nrm(ks[0], (BATCH, SEQ, D_MODEL), 1.0),
        "meta_tokens": nrm(ks[1], (N_META, D_MODEL), 1.0),
        "norm_mix": 1.0 + nrm(ks[2], (DEPTH, D_MODEL), 0.02),
        "w_in": nrm(ks[3], (DEPTH, D_MODEL, IN_PROJ), D_MODEL ** -0.5),
        "conv_w": nrm(ks[4], (DEPTH, CONV_DIM, CONV_K), CONV_K ** -0.5),
        "conv_b": nrm(ks[5], (DEPTH, CONV_DIM), 0.01),
        "dt_bias": dt0 + jnp.log(-jnp.expm1(-dt0)),
        "a_log": jnp.log(jax.random.uniform(ks[7], (DEPTH, SSM_HEADS), f, 1.0, 16.0)),
        "d_skip": 1.0 + nrm(ks[8], (DEPTH, SSM_HEADS), 0.1),
        "ssm_norm": 1.0 + nrm(ks[9], (DEPTH, SSM_D_INNER), 0.02),
        "attn_norm": 1.0 + nrm(ks[10], (DEPTH, ATTN_WIDTH), 0.02),
        "sinks": nrm(ks[11], (DEPTH, ATTN_HEADS), 0.5),
        "w_out": nrm(ks[12], (DEPTH, MIX_WIDTH, D_MODEL), MIX_WIDTH ** -0.5),
        "norm_ffn": 1.0 + nrm(ks[13], (DEPTH, D_MODEL), 0.02),
        "ffn_w1": nrm(ks[14], (N_DENSE, D_MODEL, D_FF), D_MODEL ** -0.5),
        "ffn_w3": nrm(ks[15], (N_DENSE, D_MODEL, D_FF), D_MODEL ** -0.5),
        "ffn_w2": nrm(ks[16], (N_DENSE, D_FF, D_MODEL), D_FF ** -0.5),
        "router": nrm(ks[17], (N_MOE, D_MODEL, N_EXPERTS), D_MODEL ** -0.5),
        "moe_w1": nrm(ks[18], (N_MOE, N_EXPERTS, D_MODEL, D_FF), D_MODEL ** -0.5),
        "moe_w3": nrm(ks[19], (N_MOE, N_EXPERTS, D_MODEL, D_FF), D_MODEL ** -0.5),
        "moe_w2": nrm(ks[20], (N_MOE, N_EXPERTS, D_FF, D_MODEL), D_FF ** -0.5),
        "final_norm": 1.0 + nrm(ks[21], (D_MODEL,), 0.02),
    }

def reference(x, meta_tokens, norm_mix, w_in, conv_w, conv_b, dt_bias, a_log, d_skip, ssm_norm,
              attn_norm, sinks, w_out, norm_ffn, ffn_w1, ffn_w3, ffn_w2, router, moe_w1, moe_w3,
              moe_w2, final_norm):
    bsz = x.shape[0]
    meta = jnp.broadcast_to(meta_tokens[None].astype(x.dtype), (bsz, N_META, D_MODEL))
    h = jnp.concatenate([meta, x], axis=1)
    for i in range(DEPTH):
        h = h + hybrid_mixer(rmsnorm(h, norm_mix[i]), w_in[i], conv_w[i], conv_b[i], dt_bias[i],
                             a_log[i], d_skip[i], ssm_norm[i], attn_norm[i], sinks[i], w_out[i])
        u = rmsnorm(h, norm_ffn[i])
        j = i // 2
        if i % 2 == 0:
            h = h + swiglu(u, ffn_w1[j], ffn_w3[j], ffn_w2[j])
        else:
            h = h + moe_swiglu(u, router[j], moe_w1[j], moe_w3[j], moe_w2[j])
    return rmsnorm(h, final_norm)[:, N_META:]


_drawn_inputs = setup_inputs


def setup_inputs(seed=0):
    import zlib

    import numpy as np

    out = dict(_drawn_inputs(seed))
    spreads = {}
    factors = {'conv_b': 2.835, 'sinks': 7.887, 'final_norm': 7.6, 'attn_norm': 3.748, 'norm_ffn': 2.909}
    for name, (base, spread) in spreads.items():
        noise = np.random.default_rng([zlib.crc32(name.encode()), seed]).standard_normal(out[name].shape)
        drawn = base * np.exp(spread * noise) if base else spread * noise
        out[name] = __import__('jax').numpy.asarray(drawn.astype(out[name].dtype))
    for name, factor in factors.items():
        out[name] = (out[name] * factor).astype(out[name].dtype)
    return out
```

```python
from contextlib import ExitStack

import concourse.bass as bass
from concourse import mybir

F32 = mybir.dt.float32
I32 = mybir.dt.int32
ALU = mybir.AluOpType
ACT = mybir.ActivationFunctionType
AX = mybir.AxisListType

P = 128
D = 1024
SEQ = 256
DEPTH = 2
META = 16
T = META + SEQ
KD = D // P
HEADS, KV, HD = 8, 2, 64
AW, KW = HEADS * HD, KV * HD
SH, SP_, SG, SN = 24, 64, 2, 128
DI = SH * SP_
CONV = DI + 2 * SG * SN
CK = 4
INP = AW + 2 * KW + DI + CONV + SH
MIX = AW + DI
FF = 3584
NE = 8
EPS = 1e-6
NEG = -1e30

QT, ZT, XT = AW // P, DI // P, CONV // P
FT_K, FT_V, FT_Z = QT, QT + 1, QT + 2
FT_X = FT_Z + ZT
FT_DT = FT_X + XT
MT = MIX // P
HG = SH // SG
GP = DI // SG
GT = GP // P
FT = FF // P
CH = [(0, META), (META, P), (META + P, P)]
NC = len(CH)
SLOT = 4096
WC = SLOT // KD
RING, RING_MOE = 5, 7
FC = FF // WC
WT = WC // P
MAXI = 12


IN_CHUNKS = [(4096, INP - 4096), (3584, WC), (3072, WC), (2560, WC), (2048, WC), (0, WC), (512, WC), (1024, WC),
             (1536, WC)]
OC = SLOT // MT
W2R, W2C = FF // 2, 256


def in_tiles(c0, n):
    return [(c0 + o) // P for o in range(0, n, P)]


class Rotation:

    def __init__(self, first, count, uses):
        self.first, self.count, self.uses = first, count, uses
        self.index, self.order = {}, []
        seen = {}
        for n, (name, engine) in enumerate(uses):
            assert name not in self.index, name
            k = seen.get(engine, 0)
            seen[engine] = k + 1
            self.index[name] = n
            self.order.append((engine, k + 1))
        self.total = seen

    def bank(self, name):
        return self.first + self.index[name] % self.count

    def who(self, name):
        return self.order[self.index[name]]

    def before(self, name):
        n = self.index[name] - self.count
        return self.order[n] if n >= 0 else None


def uses_a():
    u = [(("hin", t), "dve") for t in range(KD)] + [(("par",), "dve"), (("cw",), "dve"), (("dsk",), "dve")]
    for li in range(DEPTH):
        u.append((("ssq", li, 0), "act"))
        for c0, n in IN_CHUNKS:
            u += [(("proj", li, t), "act") for t in in_tiles(c0, n)]
        for g in range(SG):
            u += [(("y", li, g, j), "dve") for j in range(GT)]
        for h in range(HEADS):
            u.append((("score", li, h), "dve"))
            if h >= 1:
                u += [(("pt1", li, h - 1), "act"), (("pt2", li, h - 1), "act")]
            if h >= 2 and h % 2 == 0:
                u.append((("o", li, h // 2 - 1), "act"))
        u += [(("pt1", li, HEADS - 1), "act"), (("pt2", li, HEADS - 1), "act"), (("o", li, HEADS // 2 - 1), "act")]
        u += [(("ssqy", li, s), "act") for s in range(SG + 1)]
        u += [(("out", li, t), "dve") for t in range(KD)]
        u.append((("ssq", li, 1), "act"))
        if li == 0:
            for f in range(FT):
                u += [(("g", f), "act"), (("u", f), "dve")]
            u += [(("down", t), "dve") for t in range(KD)]
    u.append((("logit",), "dve"))
    u.append((("pos",), "dve"))
    u += [(("utm", c, r), "act") for c in range(2) for r in range(2)]
    u += [(("htm", c, r), "act") for c in range(2) for r in range(2)]
    return u


def uses_b():
    u = []
    for li in range(DEPTH):
        u.append((("small", li), "dve"))
        for g in range(SG):
            u += [(("cbt", li, g), "dve"), (("btm", li, g), "dve")]
            u += [(("xa", li, g, c, r), "dve") for c in range(NC) for r in range(2)]
            u += [(("st", li, g, c, r), "dve") for c in range(2) for r in range(2)]
    return u


def weight_loads():
    out = []
    for li in range(DEPTH):
        out += [(("in", li, n), ("proj", li, in_tiles(*IN_CHUNKS[n])[-1])) for n in range(len(IN_CHUNKS))]
        out += [(("out", li, n), ("out", li, (n + 1) * OC // P - 1)) for n in range(D // OC)]
        if li == 0:
            for c in range(FC):
                out += [(("w1", c), ("g", c * WT + WT - 1)), (("w3", c), ("u", c * WT + WT - 1))]
            out += [(("w2", q, r), ("down", q * 2 + 1)) for q in range(D // W2C) for r in range(2)]
    return out


def trunk(nc, x, meta_tokens, norm_mix, w_in, conv_w, conv_b, dt_bias, a_log, d_skip, ssm_norm, attn_norm, sinks,
          w_out, norm_ffn, ffn_w1, ffn_w3, ffn_w2, router, moe_w1, moe_w3, moe_w2, final_norm, out):
    A = Rotation(0, 4, uses_a())
    B = Rotation(4, 4, uses_b())
    loads = weight_loads()
    slot_of = {name: n % RING for n, (name, _) in enumerate(loads)}
    turn_of = {name: n // RING + 1 for n, (name, _) in enumerate(loads)}
    slot_loads = [sum(1 for n in range(len(loads)) if n % RING == s) for s in range(RING)] + [0, 0]

    acs_dram = nc.dram_tensor("acs_rows", (DEPTH, SH, T), F32, kind="Internal").ap()

    with ExitStack() as ctx:
        def sem(name):
            return ctx.enter_context(nc.semaphore(name))

        arena = ctx.enter_context(nc.sbuf_tensor("arena", [P, 53000], F32))
        top = [0]

        def take(n, at=None):
            if at is None:
                at = top[0]
                top[0] += n
                assert top[0] <= 53000, top[0]
            return arena[:, at:at + n]

        def tiles(ap, n):
            return ap.rearrange("p (a b) -> p a b", a=n)

        hT = tiles(take(KD * T), KD)
        ident = take(P)
        ones = take(P)
        NPR = 104
        par = take(NPR)
        cw = tiles(take(CK * DEPTH * XT), CK)
        mask1 = take(META + P)
        mask2 = take(META + 2 * P)
        mask_sl = take(P)
        below = take(P)
        slots_row = take(P)
        dskc = take(DEPTH * ZT)
        tri8 = tiles(take(NE * NE), NE)
        small = take(64)
        eps_c, hdt_bias, acol, dsk, sinkb = small[:, 0:1], small[:, 1:3], small[:, 3:5], small[:, 5:7], small[:, 8:24]
        rs = take(T)
        ring_at = top[0]
        ring = [take(SLOT) for _ in range(RING)]
        xn = tiles(take(KD * T), KD)
        qT = tiles(take(QT * T), QT)
        kT = tiles(take(2 * T), 2)
        vt = tiles(take(NC * KW), NC)
        over_at = top[0]
        mixT = tiles(take(MT * T), MT)
        xc = tiles(take(XT * T), XT)
        moe_at = top[0]
        AB = tiles(take(HG * T), HG)
        Wt = tiles(take(HG * T), HG)
        xdt = tiles(take(NC * GP), NC)
        xdtd = tiles(take(2 * GP), 2)
        btm = tiles(take(2 * SN), 2)
        hst = tiles(take(2 * GP), 2)
        cbt = take(T)
        raw = tiles(take(2 * (T + CK - 1)), 2)
        cacc = tiles(take(2 * T), 2)
        dtm = tiles(take(NC * 2 * SH), NC * 2)
        smax, snm, ssum, ssink, srec = [tiles(take(HEADS * NC), HEADS) for _ in range(5)]
        dl = tiles(take(2 * HG), 2)
        cdk = take(HG)
        moe_end = top[0]
        dts = [take(T, moe_at + HG * T + k * T) for k in range(8)]
        S = tiles(take(HEADS * 432, moe_at), HEADS)
        PT = tiles(take(2 * 656, moe_at + HEADS * 432), 2)
        assert HEADS * 432 + 2 * 656 <= 2 * HG * T
        hf = tiles(take(FT * T, over_at), FT)
        ring += [take(SLOT, over_at + k * SLOT) for k in range(2)]
        assert 2 * SLOT <= moe_at - over_at
        m_top = [moe_at]

        def moe(n):
            at = m_top[0]
            m_top[0] += n
            assert m_top[0] <= moe_end, (m_top[0], moe_end)
            return take(n, at)

        utm = tiles(moe(2 * D), 2)
        acc = tiles(moe(2 * D), 2)
        gfin = moe(D)
        ysb = moe(D)
        hs = tiles(moe(2 * WC), 2)
        hsT = tiles(moe(2 * WC), 2)
        xg = tiles(moe(KD * P), KD)
        sel = tiles(moe(2 * P), 2)
        selg = tiles(moe(2 * P), 2)
        selT = moe(2 * P)
        wr = tiles(moe(KD * NE), KD)
        rt = moe(400)
        fin = moe(8)
        px, cb = tiles(moe(4 * NE), 2), tiles(moe(4 * NE), 2)

        sq = tiles(take(MT * T, moe_at), MT)

        xin = tiles(take(2 * D, moe_at), 2)
        min_ = take(D, moe_at + 2 * D)
        parin = take(P, moe_at + 3 * D)
        cwin = take(CK * P, moe_at + 3 * D + P)
        sinkin = take(2 * HEADS, moe_at + 3 * D + 5 * P)

        ps = [ctx.enter_context(nc.psum_tensor(f"bank{b}", [P, 512], F32)) for b in range(8)]

        slot_loaded = [sem(f"slot_loaded{s}") for s in range(RING_MOE)]
        inputs_in = [sem(f"input_in{k}") for k in range(16)]
        a_ready = {e: sem(f"a_ready_{e}") for e in ("act", "dve")}
        a_taken = {e: sem(f"a_taken_{e}") for e in ("act", "dve")}
        b_ready, b_taken = sem("b_ready"), sem("b_taken")
        dve_step, act_step, pool_step = sem("dve_step"), sem("act_step"), sem("pool_step")
        consts_done = sem("consts_done")
        sq_ready = sem("sq_ready")
        normed = sem("normed")
        conv_done = sem("conv_done")
        xc_ready = sem("xc_ready")
        k_swapped = sem("k_swapped")
        dt_act, dt_dve = sem("dt_act"), sem("dt_dve")
        acs_ready = sem("acs_ready")
        acs_out, acs_in = sem("acs_out"), sem("acs_in")
        seg_ready = sem("seg_ready")
        dec_ready = sem("dec_ready")
        ab_exp = sem("ab_exp")
        last_dec = sem("last_dec")
        wt_ready = sem("wt_ready")
        xdtd_ready = sem("xdtd_ready")
        cdec_ready = sem("cdec_ready")
        sc_ready = sem("sc_ready")
        pexp = sem("pexp")
        p_ready = sem("p_ready")
        pt_used = sem("pt_used")
        mask_ready = sem("mask_ready")
        route_exp = sem("route_exp")
        list_ready = sem("list_ready")
        cdk_ready = sem("cdk_ready")
        gated = sem("gated")
        a_exp = sem("a_exp")
        sel_ready, gath_ready, xg_ready = sem("sel_ready"), sem("gath_ready"), sem("xg_ready")
        selt_ready, selt_taken = sem("selt_ready"), sem("selt_taken")
        g_done, u_done, g_silu, h_made = sem("g_done"), sem("u_done"), sem("g_silu"), sem("h_made")
        ht_done, ht_taken, down_done = sem("ht_done"), sem("ht_taken"), sem("down_done")
        y_taken, scat_done, scat_taken = sem("y_taken"), sem("scat_done"), sem("scat_taken")
        fin_root, out_ready, out_done = sem("fin_root"), sem("out_ready"), sem("out_done")

        block = ctx.enter_context(nc.Block())

        def emptied(eng, name, R=A):
            e, k = R.who(name)
            eng.wait_ge(a_taken[e] if R is A else b_taken, k)

        def summed(eng, stage):
            emptied(eng, [("dsk",), ("out", 0, KD - 1), ("down", KD - 1), ("out", 1, KD - 1)][stage - 1])

        def is_free(eng, name, R, taken):
            b = R.before(name)
            if b is not None:
                eng.wait_ge(taken[b[0]] if isinstance(taken, dict) else taken, b[1])

        PR_MIX, PR_FFN, PR_FIN = 0, DEPTH * KD, 2 * DEPTH * KD
        PR_SSM = PR_FIN + KD
        PR_ATT = PR_SSM + DEPTH * ZT
        PR_CB = PR_ATT + DEPTH * QT
        assert PR_CB + DEPTH * XT == NPR

        def w1_src(c, w):
            return w[:, c * WC:(c + 1) * WC].rearrange("(k p) n -> p k n", p=P)

        @block.sync
        def _(sp):
            for n, (name, _) in enumerate(loads):
                dst = ring[n % RING]
                if n >= RING:
                    e, k = A.who(loads[n - RING][1])
                    sp.wait_ge(a_ready[e], k)
                if name[0] == "in":
                    c0, nn = IN_CHUNKS[name[2]]
                    d = dst[:, 0:KD * nn].rearrange("p (k n) -> p k n", k=KD)
                    s = w_in[name[1], :, c0:c0 + nn].rearrange("(k p) n -> p k n", p=P)
                elif name[0] == "out":
                    d = dst.rearrange("p (k n) -> p k n", k=MT)
                    s = w_out[name[1], :, name[2] * OC:(name[2] + 1) * OC].rearrange("(k p) n -> p k n", p=P)
                elif name[0] in ("w1", "w3"):
                    d = dst.rearrange("p (k n) -> p k n", k=KD)
                    s = w1_src(name[1], (ffn_w1 if name[0] == "w1" else ffn_w3)[0])
                else:
                    d = dst[:, 0:FT // 2 * W2C].rearrange("p (k n) -> p k n", n=W2C)
                    s = ffn_w2[0, name[2] * W2R:(name[2] + 1) * W2R, name[1] * W2C:(name[1] + 1) * W2C]\
                        .rearrange("(k p) n -> p k n", p=P)
                sp.dma_start(d, s).then_inc(slot_loaded[n % RING], 16)

            def moe_load(k, e):
                kind, c = k % 3, k // 3
                if kind < 2:
                    w = moe_w1 if kind == 0 else moe_w3
                    s = w[0, bass.ds(e, 1), :, c * WC:(c + 1) * WC].rearrange("e (k p) n -> p (e k) n", p=P)
                    d = ring[k % RING_MOE].rearrange("p (k n) -> p k n", k=KD)
                else:
                    s = moe_w2[0, bass.ds(e, 1), c * WC:(c + 1) * WC, :].rearrange("e (k p) n -> p (e k) n", p=P)
                    d = ring[k % RING_MOE].rearrange("p (k n) -> p k n", k=WT)
                sp.dma_start(d, s).then_inc(slot_loaded[k % RING_MOE], 16)

            kinds = [g_done, u_done, down_done]
            for k in range(3 * FC):
                if k < RING:
                    last = [n for n in range(len(loads)) if n % RING == k][-1]
                    e, cnt = A.who(loads[last][1])
                    sp.wait_ge(a_ready[e], cnt)
                elif k < RING_MOE:
                    summed(sp, 4)
                else:
                    j = k - RING_MOE
                    sp.wait_ge(kinds[j % 3], j // 3 + 1)
                moe_load(k, 0)
            sp.wait_ge(list_ready, 1)
            n_items = sp.value_load(rt[0:1, 364:365].bitcast(I32), min_val=NE, max_val=MAXI - 1)
            with sp.Fori(1, n_items) as i:
                e = sp.value_load(rt[0:1, 352:364].bitcast(I32)[:, bass.ds(i, 1)], min_val=0, max_val=NE - 1)
                for k in range(3 * FC):
                    j = k - RING_MOE
                    jj = j % (3 * FC)
                    sp.wait_ge(kinds[jj % 3], i * FC + (jj // 3 + 1 - (FC if j < 0 else 0)))
                    moe_load(k, e)

        @block.tensor
        def _(pe):
            def ready(ins, name):
                ins.then_inc(a_ready[A.who(name)[0]], 1)

            def arrived(name):
                pe.wait_ge(slot_loaded[slot_of[name]], 16 * turn_of[name])

            pe.wait_ge(consts_done, 1)
            pe.wait_ge(inputs_in[0], 16)
            pe.wait_ge(inputs_in[1], 16)
            for t in range(KD):
                is_free(pe, ("hin", t), A, a_taken)
                bk = ps[A.bank(("hin", t))]
                pe.transpose(bk[:, 0:META], min_[0:META, t * P:(t + 1) * P], ident[0:META, 0:META])
                for c in range(2):
                    last = pe.transpose(bk[:, META + c * P:META + (c + 1) * P], xin[:, c, t * P:(t + 1) * P], ident)
                ready(last, ("hin", t))
            is_free(pe, ("par",), A, a_taken)
            for k in range(2, 10):
                pe.wait_ge(inputs_in[k], 16)
            ready(pe.transpose(ps[A.bank(("par",))][:, 0:NPR], parin[0:NPR, :], ident[0:NPR, 0:NPR]), ("par",))
            is_free(pe, ("cw",), A, a_taken)
            pe.wait_ge(inputs_in[10], 16)
            for w in range(CK):
                last = pe.transpose(ps[A.bank(("cw",))][:, w * 32:(w + 1) * 32],
                                    cwin[0:DEPTH * XT, w::CK], ident[0:DEPTH * XT, 0:DEPTH * XT])
            ready(last, ("cw",))
            is_free(pe, ("dsk",), A, a_taken)
            pe.wait_ge(inputs_in[11], 16)
            bk = ps[A.bank(("dsk",))]
            for j in range(ZT):
                for o in range(2):
                    h = 2 * j + o
                    last = pe.matmul(bk[64 * o:64 * o + 64, DEPTH * j:DEPTH * j + DEPTH],
                                     ident[0:SH, h:h + 1].to_broadcast([SH, 64]), dsk[0:SH, :], start=True, stop=True)
            ready(last, ("dsk",))

            def norm_sum(name, src, n, k):
                is_free(pe, name, A, a_taken)
                pe.wait_ge(sq_ready, k)
                for t in range(n):
                    last = pe.matmul(ps[A.bank(name)][:, 0:T], ones, src[:, t, :], start=(t == 0), stop=(t == n - 1))
                ready(last, name)

            NQ = 2 + SG + 1
            for li in range(DEPTH):
                norm_sum(("ssq", li, 0), xn, KD, NQ * li + 1)
                pe.wait_ge(normed, NQ * li + 1)
                for n, (c0, nn) in enumerate(IN_CHUNKS):
                    arrived(("in", li, n))
                    w = ring[slot_of[("in", li, n)]][:, 0:KD * nn].rearrange("p (k n) -> p k n", k=KD)
                    for ft in in_tiles(c0, nn):
                        name = ("proj", li, ft)
                        is_free(pe, name, A, a_taken)
                        bk = ps[A.bank(name)]
                        o = ft * P - c0
                        m = SH if ft == FT_DT else P
                        if ft == FT_V:
                            for c, (t0, L) in enumerate(CH):
                                for k in range(KD):
                                    last = pe.matmul(bk[0:L, c * P:(c + 1) * P], xn[:, k, t0:t0 + L], w[:, k, o:o + P],
                                                     start=(k == 0), stop=(k == KD - 1))
                        else:
                            for k in range(KD):
                                last = pe.matmul(bk[0:m, 0:T], w[:, k, o:o + m], xn[:, k, :],
                                                 start=(k == 0), stop=(k == KD - 1))
                        ready(last, name)
                    if n == 1:
                        name = ("small", li)
                        is_free(pe, name, B, b_taken)
                        pe.wait_ge(acs_ready, li + 1)
                        for c, (t0, L) in enumerate(CH):
                            for k, src in enumerate((dts[6], dts[7])):
                                last = pe.transpose(ps[B.bank(name)][0:L, (2 * c + k) * SH:(2 * c + k + 1) * SH],
                                                    src[0:SH, t0:t0 + L], ident[0:SH, 0:SH])
                        last.then_inc(b_ready, 1)
                pe.wait_ge(xc_ready, XT * (li + 1))
                for g in range(SG):
                    gi = li * SG + g
                    name = ("cbt", li, g)
                    is_free(pe, name, B, b_taken)
                    for c, (t0, L) in enumerate(CH):
                        last = pe.matmul(ps[B.bank(name)][0:L, t0:t0 + L], xc[:, ZT + g, t0:t0 + L],
                                         xc[:, ZT + SG + g, t0:t0 + L], start=True, stop=True)
                    last.then_inc(b_ready, 1)
                    name = ("btm", li, g)
                    is_free(pe, name, B, b_taken)
                    for c in range(2):
                        t0, L = CH[c]
                        last = pe.transpose(ps[B.bank(name)][0:L, c * P:(c + 1) * P], xc[:, ZT + g, t0:t0 + L], ident)
                    last.then_inc(b_ready, 1)
                    for c, (t0, L) in enumerate(CH):
                        for r in range(2):
                            name = ("xa", li, g, c, r)
                            is_free(pe, name, B, b_taken)
                            for j in range(3):
                                last = pe.transpose(ps[B.bank(name)][0:L, j * P:(j + 1) * P],
                                                    xc[:, GT * g + 3 * r + j, t0:t0 + L], ident)
                            last.then_inc(b_ready, 1)
                    pe.wait_ge(xdtd_ready, gi + 1)
                    for c in range(2):
                        L = CH[c][1]
                        for r in range(2):
                            name = ("st", li, g, c, r)
                            is_free(pe, name, B, b_taken)
                            pe.matmul(ps[B.bank(name)][:, 0:GP // 2], btm[0:L, c, :],
                                      xdtd[0:L, c, r * GP // 2:(r + 1) * GP // 2],
                                      start=True, stop=True).then_inc(b_ready, 1)
                    pe.wait_ge(wt_ready, gi + 1)
                    emptied(pe, ("st", li, g, 1, 1), B)
                    pe.wait_ge(cdec_ready, gi + 1)
                    for j in range(GT):
                        name = ("y", li, g, j)
                        is_free(pe, name, A, a_taken)
                        bk = ps[A.bank(name)]
                        for o in range(2):
                            h = 2 * j + o
                            for c, (t0, L) in enumerate(CH):
                                dst = bk[64 * o:64 * o + 64, t0:t0 + L]
                                last = pe.matmul(dst, xdt[0:L, c, h * 64:(h + 1) * 64], Wt[0:L, h, t0:t0 + L],
                                                 start=True, stop=(c == 0))
                                if c:
                                    last = pe.matmul(dst, hst[:, c - 1, h * 64:(h + 1) * 64], AB[:, h, t0:t0 + L],
                                                     start=False, stop=True)
                        ready(last, name)
                emptied(pe, ("proj", li, in_tiles(*IN_CHUNKS[-1])[-1]))
                pe.wait_ge(k_swapped, 32 * (li + 1))

                def score(h):
                    name = ("score", li, h)
                    is_free(pe, name, A, a_taken)
                    bk, b0 = ps[A.bank(name)], 64 * (h % 2)
                    kk = kT[b0:b0 + 64, 0 if h % 2 == h // 4 else 1, :]
                    q = qT[b0:b0 + 64, h // 2, :]
                    for c, (at, keys) in enumerate(((0, META), (META, META + P), (2 * META + P, T))):
                        t0, L = CH[c]
                        last = pe.matmul(bk[0:L, at:at + keys], q[:, t0:t0 + L], kk[:, 0:keys], start=True, stop=True)
                    ready(last, name)

                def turn(h):
                    pe.wait_ge(p_ready, HEADS * li + h + 1)
                    name = ("pt1", li, h)
                    is_free(pe, name, A, a_taken)
                    bk = ps[A.bank(name)]
                    pe.transpose(bk[0:META, 0:META], S[0:META, h, 0:META], ident[0:META, 0:META])
                    pe.transpose(bk[0:META, META:META + P], S[:, h, META:2 * META], ident)
                    ready(pe.transpose(bk[:, META + P:META + 2 * P], S[:, h, 2 * META:2 * META + P], ident), name)
                    name = ("pt2", li, h)
                    is_free(pe, name, A, a_taken)
                    bk, at = ps[A.bank(name)], 2 * META + P
                    pe.transpose(bk[0:META, 0:P], S[:, h, at:at + META], ident)
                    for c in range(2):
                        last = pe.transpose(bk[:, (1 + c) * P:(2 + c) * P],
                                            S[:, h, at + META + c * P:at + META + (c + 1) * P], ident)
                    ready(last, name)

                def weigh(h):
                    name = ("o", li, h // 2)
                    if h % 2 == 0:
                        is_free(pe, name, A, a_taken)
                    e, k = A.who(("pt2", li, h))
                    pe.wait_ge(a_taken[e], k)
                    bk, b0, g = ps[A.bank(name)], 64 * (h % 2), h // 4
                    p_ = PT[:, h % 2, :]
                    parts = [[(0, 0, META)], [(0, META, P), (1, META + P, P)],
                             [(0, META + 2 * P, P), (1, META + 3 * P, P), (2, META + 4 * P, P)]]
                    for c, (t0, L) in enumerate(CH):
                        for n, (kc, at, _) in enumerate(parts[c]):
                            kl = CH[kc][1]
                            last = pe.matmul(bk[b0:b0 + 64, t0:t0 + L], vt[0:kl, kc, g * 64:(g + 1) * 64],
                                             p_[0:kl, at:at + L], start=(n == 0), stop=(n == c))
                    if h % 2:
                        ready(last, name)
                    else:
                        last.then_inc(pt_used, 1)

                for h in range(HEADS):
                    score(h)
                    if h >= 1:
                        turn(h - 1)
                    if h >= 2 and h % 2 == 0:
                        weigh(h - 2)
                        weigh(h - 1)
                turn(HEADS - 1)
                weigh(HEADS - 2)
                weigh(HEADS - 1)
                for s, (t0, n) in enumerate([(QT, GT), (QT + GT, GT), (0, QT)]):
                    sqb = AB if s < 2 else Wt
                    norm_sum(("ssqy", li, s), tiles(arena[:, moe_at:moe_at + MT * T], MT)[:, t0:t0 + n, :], n,
                             NQ * li + 2 + s)
                pe.wait_ge(normed, NQ * li + 1 + SG + 1)
                for n in range(D // OC):
                    arrived(("out", li, n))
                    w = ring[slot_of[("out", li, n)]].rearrange("p (k n) -> p k n", k=MT)
                    for o in range(OC // P):
                        name = ("out", li, n * OC // P + o)
                        is_free(pe, name, A, a_taken)
                        for k in range(MT):
                            last = pe.matmul(ps[A.bank(name)][:, 0:T], w[:, k, o * P:(o + 1) * P], mixT[:, k, :],
                                             start=(k == 0), stop=(k == MT - 1))
                        ready(last, name)
                norm_sum(("ssq", li, 1), xn, KD, NQ * (li + 1))
                pe.wait_ge(normed, NQ * (li + 1))
                if li == 0:
                    for c in range(FC):
                        for w in ("w1", "w3"):
                            arrived((w, c))
                        for t in range(WT):
                            for w, u in (("w1", "g"), ("w3", "u")):
                                name = (u, c * WT + t)
                                is_free(pe, name, A, a_taken)
                                ws = ring[slot_of[(w, c)]].rearrange("p (k n) -> p k n", k=KD)
                                for k in range(KD):
                                    last = pe.matmul(ps[A.bank(name)][:, 0:T], ws[:, k, t * P:(t + 1) * P],
                                                     xn[:, k, :], start=(k == 0), stop=(k == KD - 1))
                                ready(last, name)
                    emptied(pe, ("u", FT - 1))
                    for q in range(D // W2C):
                        for r in range(2):
                            arrived(("w2", q, r))
                        for o in range(W2C // P):
                            name = ("down", q * 2 + o)
                            is_free(pe, name, A, a_taken)
                            for r in range(2):
                                w = ring[slot_of[("w2", q, r)]][:, 0:FT // 2 * W2C]\
                                    .rearrange("p (k n) -> p k n", n=W2C)
                                for k in range(FT // 2):
                                    last = pe.matmul(ps[A.bank(name)][:, 0:T], w[:, k, o * P:(o + 1) * P],
                                                     hf[:, r * FT // 2 + k, :], start=(r == 0 and k == 0),
                                                     stop=(r == 1 and k == FT // 2 - 1))
                            ready(last, name)
            name = ("logit",)
            is_free(pe, name, A, a_taken)
            pe.wait_ge(inputs_in[12], 16)
            for c in range(2):
                for k in range(KD):
                    last = pe.matmul(ps[A.bank(name)][:, c * NE:(c + 1) * NE],
                                     xn[:, k, META + c * P:META + (c + 1) * P], wr[:, k, :],
                                     start=(k == 0), stop=(k == KD - 1))
            ready(last, name)
            name = ("pos",)
            is_free(pe, name, A, a_taken)
            pe.wait_ge(mask_ready, 1)
            mk = rt[:, 32:48]
            bk = ps[A.bank(name)]
            pe.matmul(bk[:, 0:NE], below, mk[:, 0:NE], start=True, stop=True)
            pe.matmul(bk[:, NE:2 * NE], ones, mk[:, 0:NE], start=True, stop=False)
            pe.matmul(bk[:, NE:2 * NE], below, mk[:, NE:2 * NE], start=False, stop=True)
            pe.matmul(bk[0:1, 2 * NE:3 * NE], ones[:, 0:1], mk[:, 0:NE], start=True, stop=False)
            ready(pe.matmul(bk[0:1, 2 * NE:3 * NE], ones[:, 0:1], mk[:, NE:2 * NE], start=False, stop=True), name)
            for what, src in (("utm", xn), ("htm", hT)):
                for c in range(2):
                    for r in range(2):
                        name = (what, c, r)
                        is_free(pe, name, A, a_taken)
                        for j in range(4):
                            last = pe.transpose(ps[A.bank(name)][:, j * P:(j + 1) * P],
                                                src[:, 4 * r + j, META + c * P:META + (c + 1) * P], ident)
                        ready(last, name)
            for e in ("act", "dve"):
                pe.wait_ge(a_taken[e], A.total[e])
            pe.wait_ge(list_ready, 1)
            n_items = pe.value_load(rt[0:1, 364:365].bitcast(I32), min_val=NE, max_val=MAXI - 1)
            with pe.Fori(0, n_items) as i:
                pe.wait_ge(sel_ready, i + 1)
                for r in range(2):
                    if r == 0:
                        pe.wait_ge(scat_taken, i * 4 + 4)
                    else:
                        pe.wait_ge(xg_ready, i * 2 + 1)
                    for j in range(4):
                        for c in range(2):
                            last = pe.matmul(ps[7][:, j * P:(j + 1) * P], utm[:, c, (4 * r + j) * P:(4 * r + j + 1) * P],
                                             sel[:, c, :], start=(c == 0), stop=(c == 1))
                    last.then_inc(gath_ready, 1)
                pe.wait_ge(xg_ready, i * 2 + 2)
                for c in range(2):
                    last = pe.transpose(ps[7][:, c * P:(c + 1) * P], selg[:, c, :], ident)
                last.then_inc(selt_ready, 1)

                def loaded(k):
                    s = k % RING_MOE
                    pe.wait_ge(slot_loaded[s], i * 48 + 16 * (slot_loads[s] + k // RING_MOE + 1))
                    return ring[s]

                def up(c):
                    w = loaded(3 * c).rearrange("p (k n) -> p k n", k=KD)
                    pe.wait_ge(g_silu, i * FC + max(c + 1, 2))
                    for k in range(KD):
                        last = pe.matmul(ps[2 * (c % 2)][:, :], xg[:, k, :], w[:, k, :], start=(k == 0),
                                         stop=(k == KD - 1))
                    last.then_inc(g_done, 1)
                    w = loaded(3 * c + 1).rearrange("p (k n) -> p k n", k=KD)
                    pe.wait_ge(h_made, i * FC + max(c + 1, 2))
                    for k in range(KD):
                        last = pe.matmul(ps[2 * (c % 2) + 1][:, :], xg[:, k, :], w[:, k, :], start=(k == 0),
                                         stop=(k == KD - 1))
                    last.then_inc(u_done, 1)

                def down(c):
                    pe.wait_ge(h_made, i * FC + (c + 3))
                    pe.wait_ge(ht_taken, i * FC + (c + 1))
                    for j in range(WT):
                        last = pe.transpose(ps[4][:, j * P:(j + 1) * P], hs[:, c % 2, j * P:(j + 1) * P], ident)
                    last.then_inc(ht_done, 1)
                    w = loaded(3 * c + 2).rearrange("p (k n) -> p k n", k=WT)
                    pe.wait_ge(ht_taken, i * FC + (c + 2))
                    if c == 0:
                        pe.wait_ge(y_taken, i + 1)
                    for j in range(WT):
                        for r in range(2):
                            last = pe.matmul(ps[5 + r][:, :], hsT[:, c % 2, j * P:(j + 1) * P],
                                             w[:, j, r * WC:(r + 1) * WC], start=(c == 0 and j == 0),
                                             stop=(c == FC - 1 and j == WT - 1))
                    last.then_inc(down_done, 1)

                up(0)
                for c in range(1, FC):
                    up(c)
                    down(c - 1)
                down(FC - 1)
                pe.wait_ge(selt_taken, i + 1)
                pe.wait_ge(y_taken, i + 2)
                for n in range(4):
                    c, r = n // 2, n % 2
                    if n:
                        pe.wait_ge(scat_taken, i * 4 + 4 + n)
                    pe.matmul(ps[7][:, :], selT[:, c * P:(c + 1) * P], ysb[:, r * WC:(r + 1) * WC],
                              start=True, stop=True).then_inc(scat_done, 1)

        @block.scalar
        def _(act):
            def use(name):
                act.wait_ge(a_ready["act"], A.who(name)[1])
                assert A.who(name)[0] == "act"
                return ps[A.bank(name)]

            act.dma_start(parin[PR_MIX:PR_MIX + DEPTH * KD, :], norm_mix.rearrange("l (t p) -> (l t) p", p=P)).then_inc(inputs_in[2], 16)
            act.dma_start(parin[PR_FFN:PR_FFN + DEPTH * KD, :], norm_ffn.rearrange("l (t p) -> (l t) p", p=P)).then_inc(inputs_in[3], 16)
            act.dma_start(parin[PR_FIN:PR_FIN + KD, :], final_norm.rearrange("(t p) -> t p", p=P)).then_inc(inputs_in[4], 16)
            act.dma_start(parin[PR_SSM:PR_SSM + DEPTH * ZT, :], ssm_norm.rearrange("l (t p) -> (l t) p", p=P)).then_inc(inputs_in[5], 16)
            act.dma_start(parin[PR_ATT:PR_ATT + DEPTH * QT, :], attn_norm.rearrange("l (t p) -> (l t) p", p=P)).then_inc(inputs_in[6], 16)
            act.dma_start(parin[PR_CB:PR_CB + DEPTH * XT, :], conv_b.rearrange("l (t p) -> (l t) p", p=P)).then_inc(inputs_in[7], 16)

            n_norm = [0]

            def squares(dst, src):
                nc.scalar.activation(dst, src, ACT.Square).then_inc(sq_ready, 1)

            def root(name, n):
                if n_norm[0]:
                    act.wait_ge(normed, n_norm[0])
                n_norm[0] += 1
                nc.scalar.activation(rs, use(name)[:, 0:T], ACT.Sqrt, bias=eps_c, scale=1.0 / n)\
                    .then_inc(a_taken["act"], 1)

            act.wait_ge(inputs_in[9], 16)
            nc.scalar.activation(acol[0:SH, :], acol[0:SH, :], ACT.Exp).then_inc(a_exp, 1)
            act.wait_ge(consts_done, 1)
            for li in range(DEPTH):
                summed(act, 2 * li + 1)
                squares(xn, hT)
                root(("ssq", li, 0), D)
                xb = [0]

                def conv_silu():
                    m = xb[0]
                    n_ = li * XT + m
                    act.wait_ge(conv_done, n_ + 1)
                    ft = xorder[m]
                    nc.scalar.activation(xc[:, ft, :], cacc[:, n_ % 2, :], ACT.Silu,
                                         bias=par[:, PR_CB + li * XT + ft:PR_CB + li * XT + ft + 1])\
                        .then_inc(xc_ready, 1)
                    xb[0] += 1

                xorder = [t - FT_X for c in IN_CHUNKS for t in in_tiles(*c) if FT_X <= t < FT_DT]
                seen_x = 0
                for c0, nn in IN_CHUNKS:
                    for ft in in_tiles(c0, nn):
                        bk = use(("proj", li, ft))
                        if FT_X <= ft < FT_DT:
                            n_ = li * XT + seen_x
                            if n_ >= 2:
                                act.wait_ge(conv_done, n_ - 1)
                            nc.scalar.activation(raw[:, n_ % 2, CK - 1:CK - 1 + T], bk[:, 0:T], ACT.Identity)\
                                .then_inc(a_taken["act"], 1)
                            seen_x += 1
                            if seen_x > 1:
                                conv_silu()
                        elif ft == FT_DT:
                            nc.scalar.activation(dts[0][0:SH, :], bk[0:SH, 0:T], ACT.Identity,
                                                 bias=hdt_bias[0:SH, li:li + 1]).then_inc(a_taken["act"], 1)
                            emptied(act, ("proj", li, ft))
                            nc.scalar.activation(dts[1][0:SH, :], dts[0][0:SH, :], ACT.Abs).then_inc(dt_act, 1)
                            act.wait_ge(dt_act, 3 * li + 1)
                            nc.scalar.activation(dts[2][0:SH, :], dts[1][0:SH, :], ACT.Exp, scale=-1.0)\
                                .then_inc(dt_act, 1)
                            act.wait_ge(dt_dve, li + 1)
                            nc.scalar.activation(dts[4][0:SH, :], dts[3][0:SH, :], ACT.Ln).then_inc(dt_act, 1)
                        elif ft < FT_K:
                            nc.scalar.copy(qT[:, ft, :], bk[:, 0:T]).then_inc(a_taken["act"], 1)
                        elif ft == FT_K:
                            nc.scalar.copy(kT[:, 0, :], bk[:, 0:T]).then_inc(a_taken["act"], 1)
                        elif ft == FT_V:
                            nc.scalar.copy(vt[0:META, 0, :], bk[0:META, 0:P])
                            nc.scalar.copy(vt[:, 1:3, :], bk[:, P:3 * P].rearrange("p (a b) -> p a b", a=2))\
                                .then_inc(a_taken["act"], 1)
                        else:
                            nc.scalar.activation(mixT[:, QT + ft - FT_Z, :], bk[:, 0:T], ACT.Silu)\
                                .then_inc(a_taken["act"], 1)
                    if c0 == 2048:
                        conv_silu()
                for g in range(SG):
                    gi = li * SG + g
                    act.wait_ge(seg_ready, gi + 1)
                    nc.scalar.activation(Wt, Wt, ACT.Exp).then_inc(dec_ready, 1)
                    nc.scalar.activation(AB, AB, ACT.Exp).then_inc(ab_exp, 1)

                def exps(h):
                    k = li * HEADS + h
                    act.wait_ge(sc_ready, k + 1)
                    for c, (at, keys) in enumerate(((0, META), (META, META + P), (2 * META + P, T))):
                        L = CH[c][1]
                        nc.scalar.activation(S[0:L, h, at:at + keys], S[0:L, h, at:at + keys], ACT.Exp,
                                             bias=snm[0:L, h, c:c + 1], accum_out=ssum[0:L, h, c:c + 1])
                    nc.scalar.activation(ssink[:, h, :], snm[:, h, :], ACT.Exp,
                                         bias=sinkb[:, li * HEADS + h:li * HEADS + h + 1]).then_inc(pexp, 1)

                def take_pt(h):
                    k = li * HEADS + h
                    if h >= 2:
                        if h % 2 == 0:
                            act.wait_ge(pt_used, HEADS // 2 * li + h // 2)
                        else:
                            act.wait_ge(a_ready["act"], A.who(("o", li, (h - 2) // 2))[1])
                    bk = use(("pt1", li, h))
                    nc.scalar.copy(PT[0:META, h % 2, 0:META + P], bk[0:META, 0:META + P])
                    nc.scalar.copy(PT[:, h % 2, META + P:META + 2 * P], bk[:, META + P:META + 2 * P])\
                        .then_inc(a_taken["act"], 1)
                    bk = use(("pt2", li, h))
                    nc.scalar.copy(PT[0:META, h % 2, META + 2 * P:META + 3 * P], bk[0:META, 0:P])
                    nc.scalar.copy(PT[:, h % 2, META + 3 * P:META + 5 * P], bk[:, P:3 * P])\
                        .then_inc(a_taken["act"], 1)

                def take_o(j):
                    bk = use(("o", li, j))
                    nc.scalar.copy(mixT[:, j, :], bk[:, 0:T]).then_inc(a_taken["act"], 1)

                exps(0)
                for h in range(HEADS):
                    if h >= 1:
                        take_pt(h - 1)
                    if h >= 2 and h % 2 == 0:
                        take_o(h // 2 - 1)
                    if h + 1 < HEADS:
                        exps(h + 1)
                take_pt(HEADS - 1)
                take_o(HEADS // 2 - 1)
                emptied(act, ("o", li, HEADS // 2 - 1))
                act.wait_ge(gated, SG * GT * (li + 1))
                for t0, n in ((QT, GT), (QT + GT, GT), (0, QT)):
                    squares(sq[:, t0:t0 + n, :], mixT[:, t0:t0 + n, :])
                for s, n in enumerate((GP, GP, AW)):
                    root(("ssqy", li, s), n)
                summed(act, 2 * li + 2)
                squares(xn, hT)
                root(("ssq", li, 1), D)
                if li == 0:
                    for f in range(FT):
                        bk = use(("g", f))
                        if f >= 2:
                            emptied(act, ("u", f - 2))
                        nc.scalar.activation(cacc[:, f % 2, :], bk[:, 0:T], ACT.Silu).then_inc(a_taken["act"], 1)
            act.wait_ge(mask_ready, 2)
            nc.scalar.activation(rt[:, 48:64], rt[:, 48:64], ACT.Exp).then_inc(route_exp, 1)
            for what, dst in (("utm", utm), ("htm", acc)):
                for c in range(2):
                    for r in range(2):
                        bk = use((what, c, r))
                        nc.scalar.copy(dst[:, c, r * 512:(r + 1) * 512], bk[:, :]).then_inc(a_taken["act"], 1)
            act.sem_inc(g_silu, 2)
            act.sem_inc(ht_taken, 1)
            act.sem_inc(y_taken, 1)
            act.wait_ge(list_ready, 1)
            n_items = act.value_load(rt[0:1, 364:365].bitcast(I32), min_val=NE, max_val=MAXI - 1)
            with act.Fori(0, n_items) as i:
                for r in range(2):
                    act.wait_ge(gath_ready, i * 2 + (r + 1))
                    nc.scalar.copy(xg[:, 4 * r:4 * r + 4, :],
                                   ps[7][:, :].rearrange("p (a b) -> p a b", a=4)).then_inc(xg_ready, 1)
                act.wait_ge(selt_ready, i + 1)
                nc.scalar.copy(selT, ps[7][:, 0:2 * P]).then_inc(selt_taken, 1)

                def silu(c):
                    act.wait_ge(g_done, i * FC + (c + 1))
                    nc.scalar.activation(hs[:, c % 2, :], ps[2 * (c % 2)][:, :], ACT.Silu).then_inc(g_silu, 1)

                def take_ht(c):
                    act.wait_ge(ht_done, i * FC + (c + 1))
                    nc.scalar.copy(hsT[:, c % 2, :], ps[4][:, :]).then_inc(ht_taken, 1)

                silu(0)
                for c in range(1, FC):
                    silu(c)
                    take_ht(c - 1)
                take_ht(FC - 1)
                act.wait_ge(down_done, i * FC + FC)
                nc.scalar.copy(ysb[:, 0:WC], ps[5][:, :])
                nc.scalar.copy(ysb[:, WC:2 * WC], ps[6][:, :]).then_inc(y_taken, 1)
            act.wait_ge(scat_taken, n_items * 4 + 4)
            for c in range(2):
                nc.scalar.activation(utm[:, c, :], acc[:, c, :], ACT.Square, accum_out=fin[:, c:c + 1])\
                    .then_inc(fin_root, 1)
            act.wait_ge(fin_root, 2)
            nc.scalar.activation(fin[:, 2:4], fin[:, 0:2], ACT.Sqrt, bias=eps_c, scale=1.0 / D).then_inc(fin_root, 1)
            for c in range(2):
                act.wait_ge(out_ready, c + 1)
                act.dma_start(out[0, c * P:(c + 1) * P, :], acc[:, c, :]).then_inc(out_done, 16)
            act.wait_ge(out_done, 32)

        @block.gpsimd
        def _(pool):
            pool.dma_start(xin, x[0].rearrange("(c p) d -> p c d", p=P)).then_inc(inputs_in[0], 16)
            pool.dma_start(min_[0:META, :], meta_tokens).then_inc(inputs_in[1], 16)
            pool.dma_start(cwin[0:DEPTH * XT, :], conv_w.rearrange("l (t p) k -> (l t) (p k)", p=P)).then_inc(inputs_in[10], 16)
            pool.dma_start(hdt_bias[0:SH, :], dt_bias.rearrange("l h -> h l"), allow_slow_non_contiguous=True).then_inc(inputs_in[8], 16)
            pool.dma_start(acol[0:SH, :], a_log.rearrange("l h -> h l"), allow_slow_non_contiguous=True).then_inc(inputs_in[9], 16)
            pool.dma_start(dsk[0:SH, :], d_skip.rearrange("l h -> h l"), allow_slow_non_contiguous=True).then_inc(inputs_in[11], 16)
            pool.dma_start(sinkb[:, 0:DEPTH * HEADS], sinks.rearrange("(o l) h -> o (l h)", o=1).to_broadcast([P, DEPTH * HEADS]))\
                .then_inc(inputs_in[13], 16)
            n = [0]

            def link(ins):
                n[0] += 1
                ins.then_inc(pool_step, 1)
                pool.wait_ge(pool_step, n[0])

            def cut(ap, op, fill, step, cm, base=0):
                link(pool.affine_select(out=ap, in_=ap, compare_op=op, fill=fill, base=base,
                                        pattern=[[step, ap.shape[1]]], channel_multiplier=cm))

            link(pool.memset(ident, 0.0))
            cut(ident, ALU.not_equal, 1.0, -1, 1)
            link(pool.memset(ones, 1.0))
            link(pool.memset(eps_c, EPS))
            for t in (smax, snm, ssum, ssink):
                pool.memset(t, 1.0)
            link(pool.memset(tri8, 1.0))
            link(pool.affine_select(out=tri8, in_=tri8, compare_op=ALU.is_ge, fill=0.0, base=-1,
                                    pattern=[[1, NE], [-1, NE]], channel_multiplier=0))
            link(pool.memset(mask_sl, 0.0))
            cut(mask_sl, ALU.is_ge, NEG, 1, -1)
            link(pool.memset(mask1, 0.0))
            cut(mask1[:, META:], ALU.is_ge, NEG, -1, 1)
            link(pool.memset(mask2, 0.0))
            cut(mask2[:, META:META + P], ALU.is_ge, NEG, 1, -1, -1)
            cut(mask2[:, META + P:], ALU.is_ge, NEG, -1, 1)
            link(pool.memset(below, 1.0))
            cut(below, ALU.is_ge, 0.0, 1, -1, -1)
            link(pool.iota(cbt[:, 0:P].bitcast(I32), pattern=[[1, P]], base=0, channel_multiplier=0))
            link(pool.tensor_copy(slots_row, cbt[:, 0:P].bitcast(I32)))
            pool.memset(raw[:, :, 0:CK - 1], 0.0)
            pool.memset(cbt, 0.0).then_inc(consts_done, 1)
            for li in range(DEPTH):
                pool.wait_ge(acs_ready, li + 1)
                pool.dma_start(acs_dram[li], dts[7][0:SH, :]).then_inc(acs_out, 16)
                pool.wait_ge(acs_out, 16 * (li + 1))
                for g in range(SG):
                    gi = li * SG + g
                    if g:
                        e, k = A.who(("y", li, g - 1, GT - 1))
                        pool.wait_ge(a_ready[e], k)
                    pool.dma_start(AB.rearrange("p h t -> p (h t)"),
                                   acs_dram[li, g * HG:(g + 1) * HG, :].rearrange("(o h) t -> o (h t)", o=1).to_broadcast([P, HG * T]))\
                        .then_inc(acs_in, 16)
                    if g == 0:
                        emptied(pool, ("proj", li, FT_K))
                        pool.dma_start(kT[0:64, 1, :], kT[64:128, 0, :]).then_inc(k_swapped, 16)
                        pool.dma_start(kT[64:128, 1, :], kT[0:64, 0, :]).then_inc(k_swapped, 16)
                    pool.wait_ge(last_dec, gi + 1)
                    for c in range(2):
                        L = CH[c][1]
                        last = pool.tensor_tensor(out=xdtd[0:L, c, :].rearrange("p (h d) -> p h d", d=SP_),
                                                  in0=xdt[0:L, c, :].rearrange("p (h d) -> p h d", d=SP_),
                                                  in1=dl[0:L, c, :].unsqueeze(2).to_broadcast([L, HG, SP_]),
                                                  op=ALU.mult)
                    last.then_inc(xdtd_ready, 1)
                    pool.wait_ge(cdk_ready, gi + 1)
                    pool.tensor_tensor(out=AB[:, :, META:T], in0=AB[:, :, META:T],
                                       in1=xc[:, ZT + SG + g, META:T].unsqueeze(1).to_broadcast([P, HG, T - META]),
                                       op=ALU.mult).then_inc(cdec_ready, 1)
            summed(pool, 4)
            pool.dma_start(wr, router[0].rearrange("(k p) e -> p k e", p=P)).then_inc(inputs_in[12], 16)
            pool.dma_start(gfin, final_norm.rearrange("(o d) -> o d", o=1).to_broadcast([P, D])).then_inc(inputs_in[14], 16)
            pool.wait_ge(inputs_in[12], 16)
            pool.wait_ge(inputs_in[14], 16)

        @block.vector
        def _(dve):
            steps = [0]

            def link(ins):
                steps[0] += 1
                ins.then_inc(dve_step, 1)
                dve.wait_ge(dve_step, steps[0])

            def use(name, R=None, rdy=None):
                R = R or A
                assert R.who(name)[0] == "dve"
                dve.wait_ge(rdy or a_ready["dve"], R.who(name)[1])
                return ps[R.bank(name)]

            V = nc.vector
            dve.wait_ge(consts_done, 1)
            for t in range(KD):
                bk = use(("hin", t))
                V.tensor_copy(hT[:, t, :], bk[:, 0:T]).then_inc(a_taken["dve"], 1)
            V.tensor_copy(par, use(("par",))[:, 0:NPR]).then_inc(a_taken["dve"], 1)
            V.tensor_copy(cw.rearrange("p a b -> p (a b)"), use(("cw",))[:, 0:CK * DEPTH * XT])\
                .then_inc(a_taken["dve"], 1)
            bk = use(("dsk",))
            V.tensor_copy(dskc, bk[:, 0:DEPTH * ZT]).then_inc(a_taken["dve"], 1)
            dve.wait_ge(a_taken["dve"], A.who(("dsk",))[1])
            dve.wait_ge(a_exp, 1)
            link(V.tensor_scalar(acol[0:SH, :], acol[0:SH, :], -1.0, None, ALU.mult))

            def recip(name):
                emptied(dve, name)
                link(V.reciprocal(rs, rs))

            def scaled(dst, src, n, pc):
                for t in range(n):
                    last = V.scalar_tensor_tensor(out=dst[:, t, :], in0=src[:, t, :], scalar=par[:, pc + t:pc + t + 1],
                                                  in1=rs, op0=ALU.mult, op1=ALU.mult)
                last.then_inc(normed, 1)

            for li in range(DEPTH):
                recip(("ssq", li, 0))
                scaled(xn, hT, KD, PR_MIX + li * KD)
                xorder = [t - FT_X for c in IN_CHUNKS for t in in_tiles(*c) if FT_X <= t < FT_DT]

                def conv(m):
                    n_ = li * XT + m
                    ft = xorder[m]
                    r_ = raw[:, n_ % 2, :]
                    a_ = cacc[:, n_ % 2, :]
                    emptied(dve, ("proj", li, FT_X + ft))
                    if n_ >= 2:
                        dve.wait_ge(xc_ready, n_ - 1)
                    link(V.tensor_scalar(a_, r_[:, 0:T], cw[:, 0, li * XT + ft:li * XT + ft + 1], None, ALU.mult))
                    for w in range(1, CK):
                        ins = V.scalar_tensor_tensor(out=a_, in0=r_[:, w:w + T],
                                                     scalar=cw[:, w, li * XT + ft:li * XT + ft + 1],
                                                     in1=a_, op0=ALU.mult, op1=ALU.add)
                        if w < CK - 1:
                            link(ins)
                    ins.then_inc(conv_done, 1)

                def decay():
                    s24 = [d[0:SH, :] for d in dts]
                    dve.wait_ge(dt_act, 3 * li + 2)
                    V.tensor_scalar(s24[3], s24[2], 1.0, None, ALU.add).then_inc(dt_dve, 1)
                    dve.wait_ge(dt_dve, li + 1)
                    link(V.tensor_scalar(s24[5], s24[3], -1.0, None, ALU.add))
                    link(V.tensor_scalar(s24[1], s24[5], 0.0, None, ALU.is_equal))
                    link(V.tensor_tensor(out=s24[5], in0=s24[5], in1=s24[1], op=ALU.add))
                    link(V.reciprocal(s24[5], s24[5]))
                    link(V.tensor_tensor(out=s24[5], in0=s24[5], in1=s24[2], op=ALU.mult))
                    dve.wait_ge(dt_act, 3 * li + 3)
                    link(V.tensor_tensor(out=s24[4], in0=s24[4], in1=s24[1], op=ALU.add))
                    link(V.tensor_tensor(out=s24[5], in0=s24[5], in1=s24[4], op=ALU.mult))
                    link(V.scalar_tensor_tensor(out=s24[6], in0=s24[0], scalar=0.0, in1=s24[5], op0=ALU.max, op1=ALU.add))
                    link(V.tensor_scalar(s24[1], s24[6], acol[0:SH, li:li + 1], None, ALU.mult))
                    for c, (t0, L) in enumerate(CH):
                        last = V.tensor_tensor_scan(s24[7][:, t0:t0 + L], ones[0:SH, 0:L], s24[1][:, t0:t0 + L],
                                                    0.0, ALU.mult, ALU.add)
                    last.then_inc(acs_ready, 1)
                    bk = use(("small", li), B, b_ready)
                    V.tensor_copy(dtm[0:META, 0:2, :], bk[0:META, 0:2 * SH].rearrange("p (a b) -> p a b", a=2))
                    V.tensor_copy(dtm[:, 2:6, :], bk[:, 2 * SH:6 * SH].rearrange("p (a b) -> p a b", a=4))\
                        .then_inc(b_taken, 1)

                conv(0)
                conv(1)
                decay()
                for m in range(2, XT):
                    conv(m)
                dve.wait_ge(b_taken, B.who(("small", li))[1])
                dve.wait_ge(xc_ready, XT * (li + 1))
                for g in range(SG):
                    gi = li * SG + g
                    dve.wait_ge(acs_in, 16 * (gi + 1))
                    link(V.memset(Wt[:, :, 0:META], 0.0))
                    for h in range(HG):
                        for c, (t0, L) in enumerate(CH):
                            last = V.scalar_tensor_tensor(out=Wt[0:L, h, t0:t0 + L], in0=AB[0:L, h, t0:t0 + L],
                                                          scalar=dtm[0:L, 2 * c + 1, g * HG + h:g * HG + h + 1],
                                                          in1=mask_sl[0:L, 0:L], op0=ALU.subtract, op1=ALU.add)
                    last.then_inc(seg_ready, 1)
                    bk = use(("cbt", li, g), B, b_ready)
                    V.tensor_copy(cbt[0:META, 0:META], bk[0:META, 0:META])
                    V.tensor_copy(cbt[:, META:T], bk[:, META:T]).then_inc(b_taken, 1)
                    bk = use(("btm", li, g), B, b_ready)
                    V.tensor_copy(btm[0:META, 0, :], bk[0:META, 0:P])
                    V.tensor_copy(btm[:, 1, :], bk[:, P:2 * P]).then_inc(b_taken, 1)
                    for c, (t0, L) in enumerate(CH):
                        for r in range(2):
                            bk = use(("xa", li, g, c, r), B, b_ready)
                            hh = HG // 2
                            V.tensor_tensor(
                                out=xdt[0:L, c, r * GP // 2:(r + 1) * GP // 2].rearrange("p (h d) -> p h d", d=SP_),
                                in0=bk[0:L, 0:GP // 2].rearrange("p (h d) -> p h d", d=SP_),
                                in1=dtm[0:L, 2 * c, g * HG + r * hh:g * HG + (r + 1) * hh].unsqueeze(2)
                                .to_broadcast([L, hh, SP_]), op=ALU.mult).then_inc(b_taken, 1)
                    dve.wait_ge(b_taken, B.who(("xa", li, g, NC - 1, 1))[1])
                    dve.wait_ge(dec_ready, gi + 1)
                    V.tensor_copy(dl[0:META, 0, :], Wt[0:META, :, META - 1])
                    V.tensor_copy(dl[:, 1, :], Wt[:, :, META + P - 1]).then_inc(last_dec, 1)
                    dve.wait_ge(last_dec, gi + 1)
                    V.tensor_tensor(out=Wt, in0=Wt, in1=cbt.unsqueeze(1).to_broadcast([P, HG, T]), op=ALU.mult)\
                        .then_inc(wt_ready, 1)
                    dve.wait_ge(ab_exp, gi + 1)
                    V.tensor_copy(cdk, AB[:, :, META + P - 1]).then_inc(cdk_ready, 1)
                    dve.wait_ge(cdk_ready, gi + 1)
                    for r in range(2):
                        bk = use(("st", li, g, 0, r), B, b_ready)
                        V.tensor_copy(hst[:, 0, r * GP // 2:(r + 1) * GP // 2], bk[:, 0:GP // 2]).then_inc(b_taken, 1)
                    dve.wait_ge(b_taken, B.who(("st", li, g, 0, 1))[1])
                    link(V.tensor_tensor(out=hst[:, 1, :].rearrange("p (h d) -> p h d", d=SP_),
                                         in0=hst[:, 0, :].rearrange("p (h d) -> p h d", d=SP_),
                                         in1=cdk[:, :].unsqueeze(2).to_broadcast([P, HG, SP_]), op=ALU.mult))
                    for r in range(2):
                        bk = use(("st", li, g, 1, r), B, b_ready)
                        hh = hst[:, 1, r * GP // 2:(r + 1) * GP // 2]
                        V.tensor_tensor(out=hh, in0=hh, in1=bk[:, 0:GP // 2], op=ALU.add).then_inc(b_taken, 1)
                    for j in range(GT):
                        bk, t = use(("y", li, g, j)), GT * g + j
                        if j >= 2:
                            dve.wait_ge(gated, SG * GT * li + t - 1)
                        V.scalar_tensor_tensor(out=cacc[:, t % 2, :], in0=xc[:, t, :],
                                               scalar=dskc[:, DEPTH * t + li:DEPTH * t + li + 1], in1=bk[:, 0:T],
                                               op0=ALU.mult, op1=ALU.add).then_inc(a_taken["dve"], 1)
                        emptied(dve, ("y", li, g, j))
                        V.tensor_tensor(out=mixT[:, QT + t, :], in0=cacc[:, t % 2, :], in1=mixT[:, QT + t, :], op=ALU.mult)\
                            .then_inc(gated, 1)

                def scale_scores(h):
                    bk = use(("score", li, h))
                    masks = (mask1[0:META, META:2 * META], mask1, mask2)
                    for c, (at, keys) in enumerate(((0, META), (META, META + P), (2 * META + P, T))):
                        L = CH[c][1]
                        last = V.scalar_tensor_tensor(out=S[0:L, h, at:at + keys], in0=bk[0:L, at:at + keys],
                                                      scalar=HD ** -0.5, in1=masks[c], op0=ALU.mult, op1=ALU.add)
                    last.then_inc(a_taken["dve"], 1)
                    emptied(dve, ("score", li, h))
                    for c, (at, keys) in enumerate(((0, META), (META, META + P), (2 * META + P, T))):
                        L = CH[c][1]
                        last = V.tensor_reduce(smax[0:L, h, c:c + 1], S[0:L, h, at:at + keys], AX.X, ALU.max)
                    link(last)
                    V.tensor_scalar(snm[:, h, :], smax[:, h, :], sinkb[:, li * HEADS + h:li * HEADS + h + 1], -1.0,
                                    ALU.max, ALU.mult).then_inc(sc_ready, 1)

                def norm_scores(h):
                    dve.wait_ge(pexp, HEADS * li + h + 1)
                    link(V.tensor_tensor(out=srec[:, h, :], in0=ssum[:, h, :], in1=ssink[:, h, :], op=ALU.add))
                    link(V.reciprocal(srec[:, h, :], srec[:, h, :]))
                    for c, (at, keys) in enumerate(((0, META), (META, META + P), (2 * META + P, T))):
                        L = CH[c][1]
                        last = V.tensor_scalar(S[0:L, h, at:at + keys], S[0:L, h, at:at + keys],
                                               srec[0:L, h, c:c + 1], None, ALU.mult)
                    last.then_inc(p_ready, 1)

                dve.wait_ge(inputs_in[13], 16)
                for h in range(HEADS):
                    scale_scores(h)
                    if h:
                        norm_scores(h - 1)
                norm_scores(HEADS - 1)
                for s, (t0, n, pc) in enumerate(((QT, GT, PR_SSM + li * ZT), (QT + GT, GT, PR_SSM + li * ZT + GT),
                                                 (0, QT, PR_ATT + li * QT))):
                    recip(("ssqy", li, s))
                    scaled(mixT[:, t0:t0 + n, :], mixT[:, t0:t0 + n, :], n, pc)

                def add_residual(name, t):
                    bk = use(name)
                    V.tensor_tensor(out=hT[:, t, :], in0=hT[:, t, :], in1=bk[:, 0:T], op=ALU.add)\
                        .then_inc(a_taken["dve"], 1)

                for t in range(KD):
                    add_residual(("out", li, t), t)
                recip(("ssq", li, 1))
                scaled(xn, hT, KD, PR_FFN + li * KD)
                if li == 0:
                    for f in range(FT):
                        bk = use(("u", f))
                        emptied(dve, ("g", f))
                        V.tensor_tensor(out=hf[:, f, :], in0=cacc[:, f % 2, :], in1=bk[:, 0:T], op=ALU.mult)\
                            .then_inc(a_taken["dve"], 1)
                    for t in range(KD):
                        add_residual(("down", t), t)
            lg, mk, ea = [tiles(rt[:, o:o + 2 * NE], 2) for o in (0, 32, 48)]
            mx, sume = rt[:, 16:18], rt[:, 18:20]
            big, big2 = [rt[:, o:o + 2 * NE * NE].rearrange("p (c e j) -> p c e j", c=2, e=NE) for o in (64, 192)]
            full = [P, 2, NE, NE]
            V.tensor_copy(lg, use(("logit",))[:, 0:2 * NE].rearrange("p (c e) -> p c e", c=2)).then_inc(a_taken["dve"], 1)
            emptied(dve, ("logit",))
            own, oth = lg.unsqueeze(3).to_broadcast(full), lg.unsqueeze(2).to_broadcast(full)
            V.tensor_tensor(out=big, in0=own, in1=oth, op=ALU.is_lt)
            V.tensor_reduce(mx, lg, AX.X, ALU.max)
            link(V.tensor_tensor(out=big2, in0=own, in1=oth, op=ALU.is_equal))
            link(V.tensor_tensor(out=big2, in0=big2, in1=tri8.unsqueeze(1).to_broadcast(full), op=ALU.mult))
            link(V.tensor_tensor(out=big, in0=big, in1=big2, op=ALU.add))
            link(V.tensor_reduce(mk, big, AX.X, ALU.add))
            V.tensor_scalar(mk, mk, 1.5, None, ALU.is_lt).then_inc(mask_ready, 1)
            V.tensor_tensor(out=ea, in0=lg, in1=mx.unsqueeze(2).to_broadcast([P, 2, NE]), op=ALU.subtract)\
                .then_inc(mask_ready, 1)
            dve.wait_ge(route_exp, 1)
            link(V.tensor_tensor(out=ea, in0=ea, in1=mk, op=ALU.mult))
            link(V.tensor_reduce(sume, ea, AX.X, ALU.add))
            link(V.reciprocal(sume, sume))
            for b in range(2):
                V.tensor_tensor(out=cb[:, :, b * NE:(b + 1) * NE], in0=ea, in1=sume.unsqueeze(2).to_broadcast([P, 2, NE]),
                                op=ALU.mult)
            bk = use(("pos",))
            link(V.scalar_tensor_tensor(out=px[:, :, 0:NE], in0=bk[:, 0:2 * NE].rearrange("p (c e) -> p c e", c=2),
                                        scalar=1.0, in1=mk, op0=ALU.add, op1=ALU.mult))
            link(V.tensor_scalar(px[:, :, 0:NE], px[:, :, 0:NE], -1.0, None, ALU.add))
            link(V.tensor_scalar(px[:, :, NE:2 * NE], px[:, :, 0:NE], -float(P), None, ALU.add))
            over, incl, rk = [rt[0:1, o:o + NE] for o in (64, 72, 80)]
            lst = rt[0:1, 96:96 + 25]
            link(V.memset(lst, 0.0))
            V.tensor_copy(lst[:, 0:NE], slots_row[0:1, 0:NE])
            V.tensor_copy(lst[:, MAXI:MAXI + NE], slots_row[0:1, 0:NE])
            V.tensor_scalar(over, bk[0:1, 2 * NE:3 * NE], P + 0.5, None, ALU.is_gt).then_inc(a_taken["dve"], 1)
            emptied(dve, ("pos",))
            link(V.tensor_tensor_scan(incl, ones[0:1, 0:NE], over, 0.0, ALU.mult, ALU.add))
            link(V.tensor_tensor(out=rk, in0=incl, in1=over, op=ALU.subtract))
            link(V.tensor_scalar(lst[:, 24:25], incl[:, NE - 1:NE], float(NE), None, ALU.add))
            for j in range(MAXI - 1 - NE):
                t = rt[0:1, 128 + 8 * j:136 + 8 * j]
                link(V.scalar_tensor_tensor(out=t, in0=rk, scalar=float(j), in1=over, op0=ALU.is_equal, op1=ALU.mult))
                link(V.tensor_tensor(out=t, in0=t, in1=slots_row[0:1, 0:NE], op=ALU.mult))
                link(V.tensor_reduce(lst[:, MAXI + NE + j:MAXI + NE + j + 1], t, AX.X, ALU.add))
            link(V.tensor_scalar(lst[:, NE:MAXI - 1], lst[:, MAXI + NE:2 * MAXI - 1], float(NE), None, ALU.add))
            V.tensor_copy(rt[0:1, 340:365].bitcast(I32), lst).then_inc(list_ready, 1)
            dve.sem_inc(h_made, 2)
            dve.sem_inc(scat_taken, 4)
            dve.wait_ge(list_ready, 1)
            n_items = dve.value_load(rt[0:1, 364:365].bitcast(I32), min_val=NE, max_val=MAXI - 1)
            emptied(dve, ("htm", 1, 1))
            with dve.Fori(0, n_items) as i:
                code = dve.value_load(rt[0:1, 340:352].bitcast(I32)[:, bass.ds(i, 1)], min_val=0, max_val=2 * NE - 1)
                for c in range(2):
                    V.tensor_scalar(sel[:, c, :], slots_row, px[:, c, bass.ds(code, 1)], None, ALU.is_equal)
                    last = V.tensor_scalar(selg[:, c, :], slots_row, px[:, c, bass.ds(code, 1)],
                                           cb[:, c, bass.ds(code, 1)], ALU.is_equal, ALU.mult)
                last.then_inc(sel_ready, 1)
                for c in range(FC):
                    dve.wait_ge(g_silu, i * FC + (c + 3))
                    dve.wait_ge(u_done, i * FC + (c + 1))
                    V.tensor_tensor(out=hs[:, c % 2, :], in0=hs[:, c % 2, :], in1=ps[2 * (c % 2) + 1][:, :], op=ALU.mult)\
                        .then_inc(h_made, 1)
                for n in range(4):
                    dve.wait_ge(scat_done, i * 4 + (n + 1))
                    a_ = acc[:, n // 2, (n % 2) * WC:(n % 2 + 1) * WC]
                    V.tensor_tensor(out=a_, in0=a_, in1=ps[7][:, :], op=ALU.add).then_inc(scat_taken, 1)
            dve.wait_ge(fin_root, 3)
            link(V.reciprocal(fin[:, 4:6], fin[:, 2:4]))
            dve.wait_ge(inputs_in[14], 16)
            for c in range(2):
                V.scalar_tensor_tensor(out=acc[:, c, :], in0=acc[:, c, :], scalar=fin[:, 4 + c:5 + c], in1=gfin,
                                       op0=ALU.mult, op1=ALU.mult).then_inc(out_ready, 1)


_INS = ["x", "meta_tokens", "norm_mix", "w_in", "conv_w", "conv_b", "dt_bias", "a_log", "d_skip", "ssm_norm",
        "attn_norm", "sinks", "w_out", "norm_ffn", "ffn_w1", "ffn_w3", "ffn_w2", "router", "moe_w1", "moe_w3",
        "moe_w2", "final_norm"]


def kernel(**inputs):
    import numpy as _np
    import concourse.bacc as _bacc
    from concourse.bass_utils import run_bass_kernel_spmd as _run

    nc = _bacc.Bacc("TRN2", target_bir_lowering=False, num_devices=1)
    arrays, args = {}, []
    for name in _INS:
        a = _np.ascontiguousarray(inputs[name])
        arrays[f"in_{name}"] = a
        args.append(nc.dram_tensor(f"in_{name}", a.shape, F32, kind="ExternalInput").ap())
    args.append(nc.dram_tensor("out_0", (1, SEQ, D), F32, kind="ExternalOutput").ap())
    trunk(nc, *args)
    r = _run(nc, [arrays], core_ids=[0])
    return r.results[0]["out_0"]
```

```python
from contextlib import ExitStack

import concourse.bass as bass
from concourse import mybir

F32 = mybir.dt.float32
F32R = mybir.dt.float32r
I32 = mybir.dt.int32
ALU = mybir.AluOpType
ACT = mybir.ActivationFunctionType
AX = mybir.AxisListType

P = 128
D = 1024
SEQ = 256
DEPTH = 2
META = 16
T = META + SEQ
KD = D // P
HEADS, KV, HD = 8, 2, 64
AW, KW = HEADS * HD, KV * HD
SH, SP_, SG, SN = 24, 64, 2, 128
DI = SH * SP_
CONV = DI + 2 * SG * SN
CK = 4
INP = AW + 2 * KW + DI + CONV + SH
MIX = AW + DI
FF = 3584
NE = 8
EPS = 1e-6
NEG = -1e30

QT, ZT, XT = AW // P, DI // P, CONV // P
FT_K, FT_V, FT_Z = QT, QT + 1, QT + 2
FT_X = FT_Z + ZT
FT_DT = FT_X + XT
MT = MIX // P
HG = SH // SG
GP = DI // SG
GT = GP // P
FT = FF // P
CH = [(0, META), (META, P), (META + P, P)]
NC = len(CH)
SLOT = 4096
WC = SLOT // KD
RING = 5
KEPT = 3888
ROOM = 53000
FC = FF // WC
WT = WC // P
EC = WC // 2
EN = FF // EC
ET = EC // P
MAXI = 12


IN_CHUNKS = [(4096, INP - 4096), (3584, WC), (3072, WC), (2560, WC), (2048, WC), (0, WC), (512, WC), (1024, WC),
             (1536, WC)]
X_DONE = 4
EXP0_AFTER = 5
TURN0_AFTER = 5
ST0_AFTER = 7
Y0_AFTER = 8
OC = SLOT // MT
W2R, W2C = FF // 2, 256


def in_tiles(c0, n):
    return [(c0 + o) // P for o in range(0, n, P)]


class Rotation:

    def __init__(self, first, count, uses):
        self.first, self.count, self.uses = first, count, uses
        self.index, self.order = {}, []
        seen = {}
        for n, (name, engine) in enumerate(uses):
            assert name not in self.index, name
            k = seen.get(engine, 0)
            seen[engine] = k + 1
            self.index[name] = n
            self.order.append((engine, k + 1))
        self.total = seen

    def bank(self, name):
        return self.first + self.index[name] % self.count

    def who(self, name):
        return self.order[self.index[name]]

    def before(self, name):
        n = self.index[name] - self.count
        return self.order[n] if n >= 0 else None


def uses_a():
    u = [(("hin", t), "dve") for t in range(KD)] + [(("par",), "dve"), (("cw",), "dve"), (("dsk",), "dve")]
    for li in range(DEPTH):
        u.append((("ssq", li, 0), "act"))
        for n, chunk in enumerate(IN_CHUNKS):
            u += [(("proj", li, t), "act") for t in in_tiles(*chunk)]
            if n == Y0_AFTER:
                u += [(("y", li, 0, j), "dve") for j in range(GT)]
        for h in range(HEADS):
            u.append((("score", li, h), "dve"))
            if h >= 1:
                u += [(("pt1", li, h - 1), "act"), (("pt2", li, h - 1), "act")]
            if h >= 2 and h % 2 == 0:
                u.append((("o", li, h // 2 - 1), "act"))
        u += [(("pt1", li, HEADS - 1), "act"), (("pt2", li, HEADS - 1), "act"), (("o", li, HEADS // 2 - 1), "act")]
        u += [(("y", li, 1, j), "dve") for j in range(GT)]
        u += [(("ssqy", li, s), "act") for s in range(SG + 1)]
        u += [(("out", li, t), "dve") for t in range(KD)]
        u.append((("ssq", li, 1), "act"))
        if li == 0:
            for f in range(FT):
                u += [(("g", f), "act"), (("u", f), "dve")]
            u += [(("down", t), "dve") for t in range(KD)]
    u.append((("logit",), "dve"))
    u.append((("pos",), "dve"))
    u += [(("utm", c, r), "act") for c in range(2) for r in range(2)]
    u += [(("htm", c, r), "act") for c in range(2) for r in range(2)]
    return u


def uses_b():
    u = []
    for li in range(DEPTH):
        u.append((("small", li), "dve"))
        for g in range(SG):
            u += [(("cbt", li, g), "dve"), (("btm", li, g), "dve")]
            u += [(("xa", li, g, c, r), "dve") for c in range(NC) for r in range(2)]
            u += [(("st", li, g, c, r), "dve") for c in range(2) for r in range(2)]
    return u


def weight_loads():
    out = []
    for li in range(DEPTH):
        out += [(("in", li, n), ("proj", li, in_tiles(*IN_CHUNKS[n])[-1])) for n in range(len(IN_CHUNKS))]
        out += [(("out", li, n), ("out", li, (n + 1) * OC // P - 1)) for n in range(D // OC)]
        if li == 0:
            for c in range(FC):
                out += [(("w1", c), ("g", c * WT + WT - 1)), (("w3", c), ("u", c * WT + WT - 1))]
            out += [(("w2", q, r), ("down", q * 2 + 1)) for q in range(D // W2C) for r in range(2)]
    return out


def trunk(nc, x, meta_tokens, norm_mix, w_in, conv_w, conv_b, dt_bias, a_log, d_skip, ssm_norm, attn_norm, sinks,
          w_out, norm_ffn, ffn_w1, ffn_w3, ffn_w2, router, moe_w1, moe_w3, moe_w2, final_norm, out):
    A = Rotation(0, 4, uses_a())
    B = Rotation(4, 4, uses_b())
    loads = weight_loads()
    slot_of = {name: n % RING for n, (name, _) in enumerate(loads)}
    turn_of = {name: n // RING + 1 for n, (name, _) in enumerate(loads)}
    slot_loads = [sum(1 for n in range(len(loads)) if n % RING == s) for s in range(RING)]

    acs_dram = nc.dram_tensor("acs_rows", (DEPTH, SH, T), F32, kind="Internal").ap()

    with ExitStack() as ctx:
        def sem(name):
            return ctx.enter_context(nc.semaphore(name))

        arena_at = -(-nc.sbuf_base // 32) * 32
        SPLIT = KEPT + 3 * SLOT
        lower = ctx.enter_context(nc.sbuf_tensor("kept", [P, SPLIT], F32))
        upper = ctx.enter_context(nc.sbuf_tensor("room", [P, ROOM - SPLIT], F32))
        top = [0]

        def take(n, at=None):
            if at is None:
                at = top[0]
                top[0] += n
                assert top[0] <= ROOM, top[0]
            assert at + n <= SPLIT or at >= SPLIT
            return lower[:, at:at + n] if at < SPLIT else upper[:, at - SPLIT:at - SPLIT + n]

        def tiles(ap, n):
            return ap.rearrange("p (a b) -> p a b", a=n)

        hT = tiles(take(KD * T), KD)
        ident = take(P)
        ones = take(P)
        NPR = 104
        par = take(NPR)
        cw_at = top[0]
        cw = tiles(take(CK * DEPTH * XT), CK)
        mask1 = take(META + P)
        mask2 = take(META + 2 * P)
        mask_sl = take(P)
        below = take(P)
        slots_row = take(P)
        dskc = take(DEPTH * ZT)
        tri8 = tiles(take(NE * NE), NE)
        small = take(64)
        eps_c, hdt_bias, acol, dsk, sinkb = small[:, 0:1], small[:, 1:3], small[:, 3:5], small[:, 5:7], small[:, 8:24]
        rs = take(T)
        assert top[0] == KEPT, top[0]
        ring_at = KEPT
        ring = [take(SLOT) for _ in range(RING)]
        xn_at = top[0]
        xn = tiles(take(KD * T), KD)
        qT = tiles(take(QT * T), QT)
        kT = tiles(take(2 * T), 2)
        vt = tiles(take(NC * KW), NC)
        over_at = top[0]
        mixT = tiles(take(MT * T), MT)
        xc = tiles(take(XT * T), XT)
        moe_at = top[0]
        AB = tiles(take(HG * T), HG)
        Wt = tiles(take(HG * T), HG)
        xdt = tiles(take(NC * GP), NC)
        xdtd = tiles(take(2 * GP), 2)
        btm = tiles(take(2 * SN), 2)
        hst = tiles(take(2 * GP), 2)
        cbt = take(T)
        raw = tiles(take(2 * (T + CK - 1)), 2)
        cacc = tiles(take(2 * T), 2)
        dtm = tiles(take(NC * 2 * SH), NC * 2)
        smax, snm, ssum, ssink, srec = [tiles(take(HEADS * NC), HEADS) for _ in range(5)]
        dl = tiles(take(2 * HG), 2)
        cdk = take(HG)
        dts = [take(T, moe_at + HG * T + k * T) for k in range(8)]
        S = tiles(take(2 * 432), 2)
        PT = tiles(take(2 * 656, xn_at), 2)
        hf = tiles(take(FT * T, over_at), FT)
        m_top = [ring_at + 3 * SLOT]

        def moe(n):
            at = m_top[0]
            m_top[0] += n
            assert m_top[0] <= ROOM, m_top[0]
            return take(n, at)

        def halves(name, n):
            at = m_top[0]
            m_top[0] += n
            assert m_top[0] <= ROOM, m_top[0]
            return nc.alloc_sbuf_tensor_at(name, [P, n], F32R, offset=arena_at + 4 * at, align_bytes=4)[:, :]

        raw_w = [tiles(ring[k], 2) for k in range(3)]
        whi = [tiles(halves(f"w_high{k}", SLOT), 2) for k in range(3)]
        wlo = [tiles(halves(f"w_low{k}", SLOT), 2) for k in range(3)]
        x_at = m_top[0]
        xhi, xlo = [tiles(halves(n, KD * P), KD) for n in ("x_high", "x_low")]
        hhi, hlo = [tiles(halves(n, 2 * EC), 2) for n in ("h_high", "h_low")]
        utm = tiles(moe(2 * D), 2)
        acc = tiles(take(2 * D, 0), 2)
        gfin = utm[:, 0, :]
        ysb = take(D, x_at)
        hs = tiles(moe(2 * EC), 2)
        sel, selg = [tiles(take(2 * P, cw_at + k * 2 * P), 2) for k in range(2)]
        selT = rs[:, 0:2 * P]
        wr = tiles(moe(KD * NE), KD)
        rt = moe(400)
        fin = moe(8)
        px, cb = tiles(moe(4 * NE), 2), tiles(moe(4 * NE), 2)

        sq = tiles(take(MT * T, moe_at), MT)

        xin = tiles(take(2 * D, moe_at), 2)
        min_ = take(D, moe_at + 2 * D)
        parin = take(P, moe_at + 3 * D)
        cwin = take(CK * P, moe_at + 3 * D + P)
        sinkin = take(2 * HEADS, moe_at + 3 * D + 5 * P)

        ps = [ctx.enter_context(nc.psum_tensor(f"bank{b}", [P, 512], F32)) for b in range(8)]

        slot_loaded = [sem(f"slot_loaded{s}") for s in range(RING)]
        inputs_in = [sem(f"input_in{k}") for k in range(16)]
        a_ready = {e: sem(f"a_ready_{e}") for e in ("act", "dve")}
        a_taken = {e: sem(f"a_taken_{e}") for e in ("act", "dve")}
        b_ready, b_taken = sem("b_ready"), sem("b_taken")
        dve_step, act_step, pool_step = sem("dve_step"), sem("act_step"), sem("pool_step")
        consts_done = sem("consts_done")
        sq_ready = sem("sq_ready")
        normed = sem("normed")
        conv_done = sem("conv_done")
        xc_ready = sem("xc_ready")
        k_swapped = sem("k_swapped")
        dt_act, dt_dve = sem("dt_act"), sem("dt_dve")
        acs_ready = sem("acs_ready")
        acs_out, acs_in = sem("acs_out"), sem("acs_in")
        seg_ready = sem("seg_ready")
        dec_ready = sem("dec_ready")
        ab_exp = sem("ab_exp")
        last_dec = sem("last_dec")
        wt_ready = sem("wt_ready")
        xdtd_ready = sem("xdtd_ready")
        cdec_ready = sem("cdec_ready")
        sc_ready = sem("sc_ready")
        pexp = sem("pexp")
        p_ready = sem("p_ready")
        pt_used = sem("pt_used")
        mask_ready = sem("mask_ready")
        route_exp = sem("route_exp")
        list_ready = sem("list_ready")
        cdk_ready = sem("cdk_ready")
        gated = sem("gated")
        a_exp = sem("a_exp")
        sel_ready, gath_ready, xg_ready = sem("sel_ready"), sem("gath_ready"), sem("xg_ready")
        selt_ready, selt_taken = sem("selt_ready"), sem("selt_taken")
        g_done, u_done, g_silu, h_made = sem("g_done"), sem("u_done"), sem("g_silu"), sem("h_made")
        ht_done, ht_taken, down_done = sem("ht_done"), sem("ht_taken"), sem("down_done")
        moe_loaded = [[sem(f"moe_loaded{k}_{b}") for b in range(2)] for k in range(3)]
        hi_ready = [sem(f"hi_ready{k}") for k in range(3)]
        lo_ready = [sem(f"lo_ready{k}") for k in range(3)]
        xlo_ready, ht_low = sem("xlo_ready"), sem("ht_low")
        y_taken, scat_done, scat_taken = sem("y_taken"), sem("scat_done"), sem("scat_taken")
        fin_root, out_ready, out_done = sem("fin_root"), sem("out_ready"), sem("out_done")

        block = ctx.enter_context(nc.Block())

        def emptied(eng, name, R=A):
            e, k = R.who(name)
            eng.wait_ge(a_taken[e] if R is A else b_taken, k)

        def summed(eng, stage):
            emptied(eng, [("dsk",), ("out", 0, KD - 1), ("down", KD - 1), ("out", 1, KD - 1)][stage - 1])

        def is_free(eng, name, R, taken):
            b = R.before(name)
            if b is not None:
                eng.wait_ge(taken[b[0]] if isinstance(taken, dict) else taken, b[1])

        PR_MIX, PR_FFN, PR_FIN = 0, DEPTH * KD, 2 * DEPTH * KD
        PR_SSM = PR_FIN + KD
        PR_ATT = PR_SSM + DEPTH * ZT
        PR_CB = PR_ATT + DEPTH * QT
        assert PR_CB + DEPTH * XT == NPR

        def w1_src(c, w):
            return w[:, c * WC:(c + 1) * WC].rearrange("(k p) n -> p k n", p=P)

        @block.sync
        def _(sp):
            for n, (name, _) in enumerate(loads):
                dst = ring[n % RING]
                if n >= RING:
                    e, k = A.who(loads[n - RING][1])
                    sp.wait_ge(a_ready[e], k)
                if name[0] == "in":
                    c0, nn = IN_CHUNKS[name[2]]
                    d = dst[:, 0:KD * nn].rearrange("p (k n) -> p k n", k=KD)
                    s = w_in[name[1], :, c0:c0 + nn].rearrange("(k p) n -> p k n", p=P)
                elif name[0] == "out":
                    d = dst.rearrange("p (k n) -> p k n", k=MT)
                    s = w_out[name[1], :, name[2] * OC:(name[2] + 1) * OC].rearrange("(k p) n -> p k n", p=P)
                elif name[0] in ("w1", "w3"):
                    d = dst.rearrange("p (k n) -> p k n", k=KD)
                    s = w1_src(name[1], (ffn_w1 if name[0] == "w1" else ffn_w3)[0])
                else:
                    d = dst[:, 0:FT // 2 * W2C].rearrange("p (k n) -> p k n", n=W2C)
                    s = ffn_w2[0, name[2] * W2R:(name[2] + 1) * W2R, name[1] * W2C:(name[1] + 1) * W2C]\
                        .rearrange("(k p) n -> p k n", p=P)
                sp.dma_start(d, s).then_inc(slot_loaded[n % RING], 16)

            def moe_load(kind, c, e):
                if kind < 2:
                    w = moe_w1 if kind == 0 else moe_w3
                    s = w[0, bass.ds(e, 1), :, c * EC:(c + 1) * EC].rearrange("e (k p) n -> p (e k) n", p=P)
                    d = raw_w[kind][:, c % 2, :].rearrange("p (k n) -> p k n", k=KD)
                else:
                    s = moe_w2[0, bass.ds(e, 1), c * EC:(c + 1) * EC, :].rearrange("e (k p) n -> p (e k) n", p=P)
                    d = raw_w[kind][:, c % 2, :].rearrange("p (k n) -> p k n", k=ET)
                sp.dma_start(d, s).then_inc(moe_loaded[kind][c % 2], 16)

            for c in range(EN):
                for kind in range(3):
                    if c == 0:
                        last = [n for n in range(len(loads)) if n % RING == kind][-1]
                        e, cnt = A.who(loads[last][1])
                        sp.wait_ge(a_ready[e], cnt)
                    elif c > 1:
                        sp.wait_ge(lo_ready[kind], c - 1)
                    moe_load(kind, c, 0)
            sp.wait_ge(list_ready, 1)
            n_items = sp.value_load(rt[0:1, 364:365].bitcast(I32), min_val=NE, max_val=MAXI - 1)
            with sp.Fori(1, n_items) as i:
                e = sp.value_load(rt[0:1, 352:364].bitcast(I32)[:, bass.ds(i, 1)], min_val=0, max_val=NE - 1)
                for c in range(EN):
                    for kind in range(3):
                        sp.wait_ge(lo_ready[kind], i * EN + (c - 1))
                        moe_load(kind, c, e)
            sp.wait_ge(gath_ready, n_items * 2)
            sp.dma_start(gfin, final_norm.rearrange("(o d) -> o d", o=1).to_broadcast([P, D])).then_inc(inputs_in[14], 16)
            sp.wait_ge(inputs_in[14], 16)

        @block.tensor
        def _(pe):
            def ready(ins, name):
                ins.then_inc(a_ready[A.who(name)[0]], 1)

            def arrived(name):
                pe.wait_ge(slot_loaded[slot_of[name]], 16 * turn_of[name])

            pe.wait_ge(consts_done, 1)
            pe.wait_ge(inputs_in[0], 16)
            pe.wait_ge(inputs_in[1], 16)
            for t in range(KD):
                is_free(pe, ("hin", t), A, a_taken)
                bk = ps[A.bank(("hin", t))]
                pe.transpose(bk[:, 0:META], min_[0:META, t * P:(t + 1) * P], ident[0:META, 0:META])
                for c in range(2):
                    last = pe.transpose(bk[:, META + c * P:META + (c + 1) * P], xin[:, c, t * P:(t + 1) * P], ident)
                ready(last, ("hin", t))
            is_free(pe, ("par",), A, a_taken)
            for k in range(2, 10):
                pe.wait_ge(inputs_in[k], 16)
            ready(pe.transpose(ps[A.bank(("par",))][:, 0:NPR], parin[0:NPR, :], ident[0:NPR, 0:NPR]), ("par",))
            is_free(pe, ("cw",), A, a_taken)
            pe.wait_ge(inputs_in[10], 16)
            for w in range(CK):
                last = pe.transpose(ps[A.bank(("cw",))][:, w * 32:(w + 1) * 32],
                                    cwin[0:DEPTH * XT, w::CK], ident[0:DEPTH * XT, 0:DEPTH * XT])
            ready(last, ("cw",))
            is_free(pe, ("dsk",), A, a_taken)
            pe.wait_ge(inputs_in[11], 16)
            bk = ps[A.bank(("dsk",))]
            for j in range(ZT):
                for o in range(2):
                    h = 2 * j + o
                    last = pe.matmul(bk[64 * o:64 * o + 64, DEPTH * j:DEPTH * j + DEPTH],
                                     ident[0:SH, h:h + 1].to_broadcast([SH, 64]), dsk[0:SH, :], start=True, stop=True)
            ready(last, ("dsk",))

            def norm_sum(name, src, n, k):
                is_free(pe, name, A, a_taken)
                pe.wait_ge(sq_ready, k)
                for t in range(n):
                    last = pe.matmul(ps[A.bank(name)][:, 0:T], ones, src[:, t, :], start=(t == 0), stop=(t == n - 1))
                ready(last, name)

            NQ = 2 + SG + 1
            for li in range(DEPTH):
                norm_sum(("ssq", li, 0), xn, KD, NQ * li + 1)
                def ssd_turn(g):
                    gi = li * SG + g
                    name = ("cbt", li, g)
                    is_free(pe, name, B, b_taken)
                    for c, (t0, L) in enumerate(CH):
                        last = pe.matmul(ps[B.bank(name)][0:L, t0:t0 + L], xc[:, ZT + g, t0:t0 + L],
                                         xc[:, ZT + SG + g, t0:t0 + L], start=True, stop=True)
                    last.then_inc(b_ready, 1)
                    name = ("btm", li, g)
                    is_free(pe, name, B, b_taken)
                    for c in range(2):
                        t0, L = CH[c]
                        last = pe.transpose(ps[B.bank(name)][0:L, c * P:(c + 1) * P], xc[:, ZT + g, t0:t0 + L], ident)
                    last.then_inc(b_ready, 1)
                    for c, (t0, L) in enumerate(CH):
                        for r in range(2):
                            name = ("xa", li, g, c, r)
                            is_free(pe, name, B, b_taken)
                            for j in range(3):
                                last = pe.transpose(ps[B.bank(name)][0:L, j * P:(j + 1) * P],
                                                    xc[:, GT * g + 3 * r + j, t0:t0 + L], ident)
                            last.then_inc(b_ready, 1)

                def ssd_states(g):
                    gi = li * SG + g
                    pe.wait_ge(xdtd_ready, gi + 1)
                    for c in range(2):
                        L = CH[c][1]
                        for r in range(2):
                            name = ("st", li, g, c, r)
                            is_free(pe, name, B, b_taken)
                            pe.matmul(ps[B.bank(name)][:, 0:GP // 2], btm[0:L, c, :],
                                      xdtd[0:L, c, r * GP // 2:(r + 1) * GP // 2],
                                      start=True, stop=True).then_inc(b_ready, 1)

                def ssd_out(g):
                    gi = li * SG + g
                    pe.wait_ge(wt_ready, gi + 1)
                    emptied(pe, ("st", li, g, 1, 1), B)
                    pe.wait_ge(cdec_ready, gi + 1)
                    for j in range(GT):
                        name = ("y", li, g, j)
                        is_free(pe, name, A, a_taken)
                        bk = ps[A.bank(name)]
                        for o in range(2):
                            h = 2 * j + o
                            for c, (t0, L) in enumerate(CH):
                                dst = bk[64 * o:64 * o + 64, t0:t0 + L]
                                last = pe.matmul(dst, xdt[0:L, c, h * 64:(h + 1) * 64], Wt[0:L, h, t0:t0 + L],
                                                 start=True, stop=(c == 0))
                                if c:
                                    last = pe.matmul(dst, hst[:, c - 1, h * 64:(h + 1) * 64], AB[:, h, t0:t0 + L],
                                                     start=False, stop=True)
                        ready(last, name)

                pe.wait_ge(normed, NQ * li + 1)
                for n, (c0, nn) in enumerate(IN_CHUNKS):
                    arrived(("in", li, n))
                    w = ring[slot_of[("in", li, n)]][:, 0:KD * nn].rearrange("p (k n) -> p k n", k=KD)
                    for ft in in_tiles(c0, nn):
                        name = ("proj", li, ft)
                        is_free(pe, name, A, a_taken)
                        bk = ps[A.bank(name)]
                        o = ft * P - c0
                        m = SH if ft == FT_DT else P
                        if ft == FT_V:
                            for c, (t0, L) in enumerate(CH):
                                for k in range(KD):
                                    last = pe.matmul(bk[0:L, c * P:(c + 1) * P], xn[:, k, t0:t0 + L], w[:, k, o:o + P],
                                                     start=(k == 0), stop=(k == KD - 1))
                        else:
                            for k in range(KD):
                                last = pe.matmul(bk[0:m, 0:T], w[:, k, o:o + m], xn[:, k, :],
                                                 start=(k == 0), stop=(k == KD - 1))
                        ready(last, name)
                    if n == 1:
                        name = ("small", li)
                        is_free(pe, name, B, b_taken)
                        pe.wait_ge(acs_ready, li + 1)
                        for c, (t0, L) in enumerate(CH):
                            for k, src in enumerate((dts[6], dts[7])):
                                last = pe.transpose(ps[B.bank(name)][0:L, (2 * c + k) * SH:(2 * c + k + 1) * SH],
                                                    src[0:SH, t0:t0 + L], ident[0:SH, 0:SH])
                        last.then_inc(b_ready, 1)
                    if n == TURN0_AFTER:
                        pe.wait_ge(xc_ready, XT * (li + 1))
                        ssd_turn(0)
                    if n == ST0_AFTER:
                        ssd_states(0)
                    if n == Y0_AFTER:
                        ssd_out(0)
                        ssd_turn(1)
                emptied(pe, ("proj", li, in_tiles(*IN_CHUNKS[-1])[-1]))
                pe.wait_ge(k_swapped, 32 * (li + 1))

                def score(h):
                    name = ("score", li, h)
                    is_free(pe, name, A, a_taken)
                    bk, b0 = ps[A.bank(name)], 64 * (h % 2)
                    kk = kT[b0:b0 + 64, 0 if h % 2 == h // 4 else 1, :]
                    q = qT[b0:b0 + 64, h // 2, :]
                    for c, (at, keys) in enumerate(((0, META), (META, META + P), (2 * META + P, T))):
                        t0, L = CH[c]
                        last = pe.matmul(bk[0:L, at:at + keys], q[:, t0:t0 + L], kk[:, 0:keys], start=True, stop=True)
                    ready(last, name)

                def turn(h):
                    pe.wait_ge(p_ready, HEADS * li + h + 1)
                    name = ("pt1", li, h)
                    is_free(pe, name, A, a_taken)
                    bk = ps[A.bank(name)]
                    pe.transpose(bk[0:META, 0:META], S[0:META, h % 2, 0:META], ident[0:META, 0:META])
                    pe.transpose(bk[0:META, META:META + P], S[:, h % 2, META:2 * META], ident)
                    ready(pe.transpose(bk[:, META + P:META + 2 * P], S[:, h % 2, 2 * META:2 * META + P], ident), name)
                    name = ("pt2", li, h)
                    is_free(pe, name, A, a_taken)
                    bk, at = ps[A.bank(name)], 2 * META + P
                    pe.transpose(bk[0:META, 0:P], S[:, h % 2, at:at + META], ident)
                    for c in range(2):
                        last = pe.transpose(bk[:, (1 + c) * P:(2 + c) * P],
                                            S[:, h % 2, at + META + c * P:at + META + (c + 1) * P], ident)
                    ready(last, name)

                def weigh(h):
                    name = ("o", li, h // 2)
                    if h % 2 == 0:
                        is_free(pe, name, A, a_taken)
                    e, k = A.who(("pt2", li, h))
                    pe.wait_ge(a_taken[e], k)
                    bk, b0, g = ps[A.bank(name)], 64 * (h % 2), h // 4
                    p_ = PT[:, h % 2, :]
                    parts = [[(0, 0, META)], [(0, META, P), (1, META + P, P)],
                             [(0, META + 2 * P, P), (1, META + 3 * P, P), (2, META + 4 * P, P)]]
                    for c, (t0, L) in enumerate(CH):
                        for n, (kc, at, _) in enumerate(parts[c]):
                            kl = CH[kc][1]
                            last = pe.matmul(bk[b0:b0 + 64, t0:t0 + L], vt[0:kl, kc, g * 64:(g + 1) * 64],
                                             p_[0:kl, at:at + L], start=(n == 0), stop=(n == c))
                    if h % 2:
                        ready(last, name)
                    else:
                        last.then_inc(pt_used, 1)

                for h in range(HEADS):
                    score(h)
                    if h >= 1:
                        turn(h - 1)
                    if h >= 2 and h % 2 == 0:
                        weigh(h - 2)
                        weigh(h - 1)
                turn(HEADS - 1)
                weigh(HEADS - 2)
                weigh(HEADS - 1)
                ssd_states(1)
                ssd_out(1)
                for s, (t0, n) in enumerate([(QT, GT), (QT + GT, GT), (0, QT)]):
                    sqb = AB if s < 2 else Wt
                    norm_sum(("ssqy", li, s), sq[:, t0:t0 + n, :], n,
                             NQ * li + 2 + s)
                pe.wait_ge(normed, NQ * li + 1 + SG + 1)
                for n in range(D // OC):
                    arrived(("out", li, n))
                    w = ring[slot_of[("out", li, n)]].rearrange("p (k n) -> p k n", k=MT)
                    for o in range(OC // P):
                        name = ("out", li, n * OC // P + o)
                        is_free(pe, name, A, a_taken)
                        for k in range(MT):
                            last = pe.matmul(ps[A.bank(name)][:, 0:T], w[:, k, o * P:(o + 1) * P], mixT[:, k, :],
                                             start=(k == 0), stop=(k == MT - 1))
                        ready(last, name)
                norm_sum(("ssq", li, 1), xn, KD, NQ * (li + 1))
                pe.wait_ge(normed, NQ * (li + 1))
                if li == 0:
                    for c in range(FC):
                        for w in ("w1", "w3"):
                            arrived((w, c))
                        for t in range(WT):
                            for w, u in (("w1", "g"), ("w3", "u")):
                                name = (u, c * WT + t)
                                is_free(pe, name, A, a_taken)
                                ws = ring[slot_of[(w, c)]].rearrange("p (k n) -> p k n", k=KD)
                                for k in range(KD):
                                    last = pe.matmul(ps[A.bank(name)][:, 0:T], ws[:, k, t * P:(t + 1) * P],
                                                     xn[:, k, :], start=(k == 0), stop=(k == KD - 1))
                                ready(last, name)
                    emptied(pe, ("u", FT - 1))
                    for q in range(D // W2C):
                        for r in range(2):
                            arrived(("w2", q, r))
                        for o in range(W2C // P):
                            name = ("down", q * 2 + o)
                            is_free(pe, name, A, a_taken)
                            for r in range(2):
                                w = ring[slot_of[("w2", q, r)]][:, 0:FT // 2 * W2C]\
                                    .rearrange("p (k n) -> p k n", n=W2C)
                                for k in range(FT // 2):
                                    last = pe.matmul(ps[A.bank(name)][:, 0:T], w[:, k, o * P:(o + 1) * P],
                                                     hf[:, r * FT // 2 + k, :], start=(r == 0 and k == 0),
                                                     stop=(r == 1 and k == FT // 2 - 1))
                            ready(last, name)
            name = ("logit",)
            is_free(pe, name, A, a_taken)
            pe.wait_ge(inputs_in[12], 16)
            for c in range(2):
                for k in range(KD):
                    last = pe.matmul(ps[A.bank(name)][:, c * NE:(c + 1) * NE],
                                     xn[:, k, META + c * P:META + (c + 1) * P], wr[:, k, :],
                                     start=(k == 0), stop=(k == KD - 1))
            ready(last, name)
            name = ("pos",)
            is_free(pe, name, A, a_taken)
            pe.wait_ge(mask_ready, 1)
            mk = rt[:, 32:48]
            bk = ps[A.bank(name)]
            pe.matmul(bk[:, 0:NE], below, mk[:, 0:NE], start=True, stop=True)
            pe.matmul(bk[:, NE:2 * NE], ones, mk[:, 0:NE], start=True, stop=False)
            pe.matmul(bk[:, NE:2 * NE], below, mk[:, NE:2 * NE], start=False, stop=True)
            pe.matmul(bk[0:1, 2 * NE:3 * NE], ones[:, 0:1], mk[:, 0:NE], start=True, stop=False)
            ready(pe.matmul(bk[0:1, 2 * NE:3 * NE], ones[:, 0:1], mk[:, NE:2 * NE], start=False, stop=True), name)
            for what, src in (("utm", xn), ("htm", hT)):
                for c in range(2):
                    for r in range(2):
                        name = (what, c, r)
                        is_free(pe, name, A, a_taken)
                        for j in range(4):
                            last = pe.transpose(ps[A.bank(name)][:, j * P:(j + 1) * P],
                                                src[:, 4 * r + j, META + c * P:META + (c + 1) * P], ident)
                        ready(last, name)
            for e in ("act", "dve"):
                pe.wait_ge(a_taken[e], A.total[e])
            for k in (g_done, u_done, down_done):
                pe.sem_inc(k, 2)
            pe.wait_ge(list_ready, 1)
            n_items = pe.value_load(rt[0:1, 364:365].bitcast(I32), min_val=NE, max_val=MAXI - 1)
            with pe.Fori(0, n_items) as i:
                pe.wait_ge(sel_ready, i + 1)
                for r in range(2):
                    bk = ps[(7, 4)[r]]
                    for j in range(4):
                        for c in range(2):
                            last = pe.matmul(bk[:, j * P:(j + 1) * P], utm[:, c, (4 * r + j) * P:(4 * r + j + 1) * P],
                                             sel[:, c, :], start=(c == 0), stop=(c == 1))
                    last.then_inc(gath_ready, 1)
                pe.wait_ge(xlo_ready, i * 2 + 2)
                for c in range(2):
                    last = pe.transpose(ps[7][:, c * P:(c + 1) * P], selg[:, c, :], ident)
                last.then_inc(selt_ready, 1)
                pe.wait_ge(scat_taken, i * 4 + 4)

                def up(kind, c):
                    bk, free, done = ((ps[2 * (c % 2)], g_silu, g_done), (ps[2 * (c % 2) + 1], h_made, u_done))[kind]
                    pe.wait_ge(lo_ready[kind], i * EN + (c + 1))
                    pe.wait_ge(free, i * EN + (c + 1))
                    wh, wl = [w[kind][:, c % 2, :].rearrange("p (k n) -> p k n", k=KD) for w in (whi, wlo)]
                    for k in range(KD):
                        pe.matmul(bk[:, 0:EC], xhi[:, k, :], wh[:, k, :], start=(k == 0), stop=False)
                        pe.matmul(bk[:, 0:EC], xhi[:, k, :], wl[:, k, :], start=False, stop=False)
                        last = pe.matmul(bk[:, 0:EC], xlo[:, k, :], wh[:, k, :], start=False, stop=(k == KD - 1))
                    last.then_inc(done, 1)

                def turn_h(c):
                    pe.wait_ge(h_made, i * EN + (c + 3))
                    pe.wait_ge(ht_low, i * EN + (c + 1))
                    for j in range(ET):
                        last = pe.transpose(ps[4][:, j * P:(j + 1) * P], hs[:, c % 2, j * P:(j + 1) * P], ident)
                    last.then_inc(ht_done, 1)

                def down(c):
                    pe.wait_ge(lo_ready[2], i * EN + (c + 1))
                    pe.wait_ge(ht_low, i * EN + (c + 2))
                    if c == 0:
                        pe.wait_ge(y_taken, i + 1)
                    wh, wl = [w[2][:, c % 2, :].rearrange("p (k n) -> p k n", k=ET) for w in (whi, wlo)]
                    for j in range(ET):
                        for h_, w_, n in ((hhi, wh, 0), (hhi, wl, 1), (hlo, wh, 2)):
                            for r in range(2):
                                last = pe.matmul(ps[5 + r][:, :], h_[:, c % 2, j * P:(j + 1) * P],
                                                 w_[:, j, r * WC:(r + 1) * WC], start=(c == 0 and j == 0 and n == 0),
                                                 stop=(c == EN - 1 and j == ET - 1 and n == 2))
                    last.then_inc(down_done, 1)

                for c in range(EN):
                    up(0, c)
                    if c:
                        turn_h(c - 1)
                    up(1, c)
                    if c:
                        down(c - 1)
                turn_h(EN - 1)
                down(EN - 1)
                pe.wait_ge(selt_taken, i + 1)
                pe.wait_ge(y_taken, i + 2)
                for n in range(4):
                    c, r = n // 2, n % 2
                    pe.matmul(ps[n][:, :], selT[:, c * P:(c + 1) * P], ysb[:, r * WC:(r + 1) * WC],
                              start=True, stop=True).then_inc(scat_done, 1)

        @block.scalar
        def _(act):
            def use(name):
                act.wait_ge(a_ready["act"], A.who(name)[1])
                assert A.who(name)[0] == "act"
                return ps[A.bank(name)]

            act.dma_start(parin[PR_MIX:PR_MIX + DEPTH * KD, :], norm_mix.rearrange("l (t p) -> (l t) p", p=P)).then_inc(inputs_in[2], 16)
            act.dma_start(parin[PR_FFN:PR_FFN + DEPTH * KD, :], norm_ffn.rearrange("l (t p) -> (l t) p", p=P)).then_inc(inputs_in[3], 16)
            act.dma_start(parin[PR_FIN:PR_FIN + KD, :], final_norm.rearrange("(t p) -> t p", p=P)).then_inc(inputs_in[4], 16)
            act.dma_start(parin[PR_SSM:PR_SSM + DEPTH * ZT, :], ssm_norm.rearrange("l (t p) -> (l t) p", p=P)).then_inc(inputs_in[5], 16)
            act.dma_start(parin[PR_ATT:PR_ATT + DEPTH * QT, :], attn_norm.rearrange("l (t p) -> (l t) p", p=P)).then_inc(inputs_in[6], 16)
            act.dma_start(parin[PR_CB:PR_CB + DEPTH * XT, :], conv_b.rearrange("l (t p) -> (l t) p", p=P)).then_inc(inputs_in[7], 16)

            n_norm = [0]

            def squares(dst, src):
                nc.scalar.activation(dst, src, ACT.Square).then_inc(sq_ready, 1)

            def root(name, n):
                if n_norm[0]:
                    act.wait_ge(normed, n_norm[0])
                n_norm[0] += 1
                nc.scalar.activation(rs, use(name)[:, 0:T], ACT.Sqrt, bias=eps_c, scale=1.0 / n)\
                    .then_inc(a_taken["act"], 1)

            act.wait_ge(inputs_in[9], 16)
            nc.scalar.activation(acol[0:SH, :], acol[0:SH, :], ACT.Exp).then_inc(a_exp, 1)
            act.wait_ge(consts_done, 1)
            for li in range(DEPTH):
                summed(act, 2 * li + 1)
                squares(xn, hT)
                root(("ssq", li, 0), D)
                xb = [0]

                def conv_silu():
                    m = xb[0]
                    n_ = li * XT + m
                    act.wait_ge(conv_done, n_ + 1)
                    ft = xorder[m]
                    nc.scalar.activation(xc[:, ft, :], cacc[:, n_ % 2, :], ACT.Silu,
                                         bias=par[:, PR_CB + li * XT + ft:PR_CB + li * XT + ft + 1])\
                        .then_inc(xc_ready, 1)
                    xb[0] += 1

                xorder = [t - FT_X for c in IN_CHUNKS for t in in_tiles(*c) if FT_X <= t < FT_DT]
                seen_x = 0

                def decays(g):
                    act.wait_ge(seg_ready, li * SG + g + 1)
                    nc.scalar.activation(Wt, Wt, ACT.Exp).then_inc(dec_ready, 1)
                    nc.scalar.activation(AB, AB, ACT.Exp).then_inc(ab_exp, 1)

                for n, (c0, nn) in enumerate(IN_CHUNKS):
                    for ft in in_tiles(c0, nn):
                        bk = use(("proj", li, ft))
                        if FT_X <= ft < FT_DT:
                            n_ = li * XT + seen_x
                            if n_ >= 2:
                                act.wait_ge(conv_done, n_ - 1)
                            nc.scalar.activation(raw[:, n_ % 2, CK - 1:CK - 1 + T], bk[:, 0:T], ACT.Identity)\
                                .then_inc(a_taken["act"], 1)
                            seen_x += 1
                            if seen_x > 1:
                                conv_silu()
                        elif ft == FT_DT:
                            nc.scalar.activation(dts[0][0:SH, :], bk[0:SH, 0:T], ACT.Identity,
                                                 bias=hdt_bias[0:SH, li:li + 1]).then_inc(a_taken["act"], 1)
                            emptied(act, ("proj", li, ft))
                            nc.scalar.activation(dts[1][0:SH, :], dts[0][0:SH, :], ACT.Abs).then_inc(dt_act, 1)
                            act.wait_ge(dt_act, 3 * li + 1)
                            nc.scalar.activation(dts[2][0:SH, :], dts[1][0:SH, :], ACT.Exp, scale=-1.0)\
                                .then_inc(dt_act, 1)
                            act.wait_ge(dt_dve, li + 1)
                            nc.scalar.activation(dts[4][0:SH, :], dts[3][0:SH, :], ACT.Ln).then_inc(dt_act, 1)
                        elif ft < FT_K:
                            nc.scalar.copy(qT[:, ft, :], bk[:, 0:T]).then_inc(a_taken["act"], 1)
                        elif ft == FT_K:
                            nc.scalar.copy(kT[:, 0, :], bk[:, 0:T]).then_inc(a_taken["act"], 1)
                        elif ft == FT_V:
                            nc.scalar.copy(vt[0:META, 0, :], bk[0:META, 0:P])
                            nc.scalar.copy(vt[:, 1:3, :], bk[:, P:3 * P].rearrange("p (a b) -> p a b", a=2))\
                                .then_inc(a_taken["act"], 1)
                        else:
                            nc.scalar.activation(mixT[:, QT + ft - FT_Z, :], bk[:, 0:T], ACT.Silu)\
                                .then_inc(a_taken["act"], 1)
                    if n == X_DONE:
                        conv_silu()
                    if n == EXP0_AFTER:
                        decays(0)
                decays(1)

                def exps(h):
                    k = li * HEADS + h
                    act.wait_ge(sc_ready, k + 1)
                    for c, (at, keys) in enumerate(((0, META), (META, META + P), (2 * META + P, T))):
                        L = CH[c][1]
                        nc.scalar.activation(S[0:L, h % 2, at:at + keys], S[0:L, h % 2, at:at + keys], ACT.Exp,
                                             bias=snm[0:L, h, c:c + 1], accum_out=ssum[0:L, h, c:c + 1])
                    nc.scalar.activation(ssink[:, h, :], snm[:, h, :], ACT.Exp,
                                         bias=sinkb[:, li * HEADS + h:li * HEADS + h + 1]).then_inc(pexp, 1)

                def take_pt(h):
                    k = li * HEADS + h
                    if h >= 2:
                        if h % 2 == 0:
                            act.wait_ge(pt_used, HEADS // 2 * li + h // 2)
                        else:
                            act.wait_ge(a_ready["act"], A.who(("o", li, (h - 2) // 2))[1])
                    bk = use(("pt1", li, h))
                    nc.scalar.copy(PT[0:META, h % 2, 0:META + P], bk[0:META, 0:META + P])
                    nc.scalar.copy(PT[:, h % 2, META + P:META + 2 * P], bk[:, META + P:META + 2 * P])\
                        .then_inc(a_taken["act"], 1)
                    bk = use(("pt2", li, h))
                    nc.scalar.copy(PT[0:META, h % 2, META + 2 * P:META + 3 * P], bk[0:META, 0:P])
                    nc.scalar.copy(PT[:, h % 2, META + 3 * P:META + 5 * P], bk[:, P:3 * P])\
                        .then_inc(a_taken["act"], 1)

                def take_o(j):
                    bk = use(("o", li, j))
                    nc.scalar.copy(mixT[:, j, :], bk[:, 0:T]).then_inc(a_taken["act"], 1)

                exps(0)
                for h in range(HEADS):
                    if h >= 1:
                        take_pt(h - 1)
                    if h >= 2 and h % 2 == 0:
                        take_o(h // 2 - 1)
                    if h + 1 < HEADS:
                        exps(h + 1)
                take_pt(HEADS - 1)
                take_o(HEADS // 2 - 1)
                emptied(act, ("o", li, HEADS // 2 - 1))
                act.wait_ge(gated, SG * GT * (li + 1))
                for t0, n in ((QT, GT), (QT + GT, GT), (0, QT)):
                    squares(sq[:, t0:t0 + n, :], mixT[:, t0:t0 + n, :])
                for s, n in enumerate((GP, GP, AW)):
                    root(("ssqy", li, s), n)
                summed(act, 2 * li + 2)
                squares(xn, hT)
                root(("ssq", li, 1), D)
                if li == 0:
                    for f in range(FT):
                        bk = use(("g", f))
                        if f >= 2:
                            emptied(act, ("u", f - 2))
                        nc.scalar.activation(cacc[:, f % 2, :], bk[:, 0:T], ACT.Silu).then_inc(a_taken["act"], 1)
            act.wait_ge(mask_ready, 2)
            nc.scalar.activation(rt[:, 48:64], rt[:, 48:64], ACT.Exp).then_inc(route_exp, 1)
            for what, dst in (("utm", utm), ("htm", acc)):
                act.wait_ge(a_ready["act"], A.who((what, 1, 1))[1])
                for c in range(2):
                    for r in range(2):
                        bk = use((what, c, r))
                        nc.scalar.copy(dst[:, c, r * 512:(r + 1) * 512], bk[:, :]).then_inc(a_taken["act"], 1)
            act.sem_inc(g_silu, 2)
            act.sem_inc(y_taken, 1)
            act.wait_ge(list_ready, 1)
            emptied(act, ("out", DEPTH - 1, KD - 1))
            n_items = act.value_load(rt[0:1, 364:365].bitcast(I32), min_val=NE, max_val=MAXI - 1)
            with act.Fori(0, n_items) as i:
                def high(kind, c):
                    act.wait_ge(moe_loaded[kind][c % 2], i * (8 * EN) + 16 * (c // 2 + 1))
                    act.wait_ge((g_done, u_done, down_done)[kind], i * EN + (c + 1))
                    nc.scalar.copy(whi[kind][:, c % 2, :], raw_w[kind][:, c % 2, :]).then_inc(hi_ready[kind], 1)

                def silu(c):
                    act.wait_ge(g_done, i * EN + (c + 3))
                    nc.scalar.activation(hs[:, c % 2, :], ps[2 * (c % 2)][:, 0:EC], ACT.Silu).then_inc(g_silu, 1)

                def high_h(c):
                    act.wait_ge(ht_done, i * EN + (c + 1))
                    nc.scalar.copy(hhi[:, c % 2, :], ps[4][:, 0:EC]).then_inc(ht_taken, 1)

                high(0, 0)
                for r in range(2):
                    act.wait_ge(gath_ready, i * 2 + (r + 1))
                    nc.scalar.copy(xhi[:, 4 * r:4 * r + 4, :],
                                   ps[(7, 4)[r]][:, :].rearrange("p (a b) -> p a b", a=4)).then_inc(xg_ready, 1)
                high(1, 0)
                act.wait_ge(selt_ready, i + 1)
                nc.scalar.copy(selT, ps[7][:, 0:2 * P]).then_inc(selt_taken, 1)
                for c in range(EN):
                    silu(c)
                    if c:
                        high_h(c - 1)
                    if c + 1 < EN:
                        high(0, c + 1)
                        high(1, c + 1)
                    high(2, c)
                high_h(EN - 1)
                act.wait_ge(down_done, i * EN + (EN + 2))
                nc.scalar.copy(ysb[:, 0:WC], ps[5][:, :])
                nc.scalar.copy(ysb[:, WC:2 * WC], ps[6][:, :]).then_inc(y_taken, 1)
            act.wait_ge(scat_taken, n_items * 4 + 4)
            for c in range(2):
                nc.scalar.activation((ysb, utm[:, 1, :])[c], acc[:, c, :], ACT.Square, accum_out=fin[:, c:c + 1])\
                    .then_inc(fin_root, 1)
            act.wait_ge(fin_root, 2)
            nc.scalar.activation(fin[:, 2:4], fin[:, 0:2], ACT.Sqrt, bias=eps_c, scale=1.0 / D).then_inc(fin_root, 1)
            for c in range(2):
                act.wait_ge(out_ready, c + 1)
                act.dma_start(out[0, c * P:(c + 1) * P, :], acc[:, c, :]).then_inc(out_done, 16)
            act.wait_ge(out_done, 32)

        @block.gpsimd
        def _(pool):
            pool.dma_start(xin, x[0].rearrange("(c p) d -> p c d", p=P)).then_inc(inputs_in[0], 16)
            pool.dma_start(min_[0:META, :], meta_tokens).then_inc(inputs_in[1], 16)
            pool.dma_start(cwin[0:DEPTH * XT, :], conv_w.rearrange("l (t p) k -> (l t) (p k)", p=P)).then_inc(inputs_in[10], 16)
            pool.dma_start(hdt_bias[0:SH, :], dt_bias.rearrange("l h -> h l"), allow_slow_non_contiguous=True).then_inc(inputs_in[8], 16)
            pool.dma_start(acol[0:SH, :], a_log.rearrange("l h -> h l"), allow_slow_non_contiguous=True).then_inc(inputs_in[9], 16)
            pool.dma_start(dsk[0:SH, :], d_skip.rearrange("l h -> h l"), allow_slow_non_contiguous=True).then_inc(inputs_in[11], 16)
            pool.dma_start(sinkb[:, 0:DEPTH * HEADS], sinks.rearrange("(o l) h -> o (l h)", o=1).to_broadcast([P, DEPTH * HEADS]))\
                .then_inc(inputs_in[13], 16)
            n = [0]

            def link(ins):
                n[0] += 1
                ins.then_inc(pool_step, 1)
                pool.wait_ge(pool_step, n[0])

            def cut(ap, op, fill, step, cm, base=0):
                link(pool.affine_select(out=ap, in_=ap, compare_op=op, fill=fill, base=base,
                                        pattern=[[step, ap.shape[1]]], channel_multiplier=cm))

            link(pool.memset(ident, 0.0))
            cut(ident, ALU.not_equal, 1.0, -1, 1)
            link(pool.memset(ones, 1.0))
            link(pool.memset(eps_c, EPS))
            for t in (smax, snm, ssum, ssink):
                pool.memset(t, 1.0)
            link(pool.memset(tri8, 1.0))
            link(pool.affine_select(out=tri8, in_=tri8, compare_op=ALU.is_ge, fill=0.0, base=-1,
                                    pattern=[[1, NE], [-1, NE]], channel_multiplier=0))
            link(pool.memset(mask_sl, 0.0))
            cut(mask_sl, ALU.is_ge, NEG, 1, -1)
            link(pool.memset(mask1, 0.0))
            cut(mask1[:, META:], ALU.is_ge, NEG, -1, 1)
            link(pool.memset(mask2, 0.0))
            cut(mask2[:, META:META + P], ALU.is_ge, NEG, 1, -1, -1)
            cut(mask2[:, META + P:], ALU.is_ge, NEG, -1, 1)
            link(pool.memset(below, 1.0))
            cut(below, ALU.is_ge, 0.0, 1, -1, -1)
            link(pool.iota(cbt[:, 0:P].bitcast(I32), pattern=[[1, P]], base=0, channel_multiplier=0))
            link(pool.tensor_copy(slots_row, cbt[:, 0:P].bitcast(I32)))
            pool.memset(raw[:, :, 0:CK - 1], 0.0)
            pool.memset(cbt, 0.0).then_inc(consts_done, 1)
            for li in range(DEPTH):
                pool.wait_ge(acs_ready, li + 1)
                pool.dma_start(acs_dram[li], dts[7][0:SH, :]).then_inc(acs_out, 16)
                pool.wait_ge(acs_out, 16 * (li + 1))
                for g in range(SG):
                    gi = li * SG + g
                    if g:
                        e, k = A.who(("y", li, g - 1, GT - 1))
                        pool.wait_ge(a_ready[e], k)
                    pool.dma_start(AB.rearrange("p h t -> p (h t)"),
                                   acs_dram[li, g * HG:(g + 1) * HG, :].rearrange("(o h) t -> o (h t)", o=1).to_broadcast([P, HG * T]))\
                        .then_inc(acs_in, 16)
                    if g == 0:
                        emptied(pool, ("proj", li, FT_K))
                        pool.dma_start(kT[0:64, 1, :], kT[64:128, 0, :]).then_inc(k_swapped, 16)
                        pool.dma_start(kT[64:128, 1, :], kT[0:64, 0, :]).then_inc(k_swapped, 16)
                    pool.wait_ge(last_dec, gi + 1)
                    for c in range(2):
                        L = CH[c][1]
                        last = pool.tensor_tensor(out=xdtd[0:L, c, :].rearrange("p (h d) -> p h d", d=SP_),
                                                  in0=xdt[0:L, c, :].rearrange("p (h d) -> p h d", d=SP_),
                                                  in1=dl[0:L, c, :].unsqueeze(2).to_broadcast([L, HG, SP_]),
                                                  op=ALU.mult)
                    last.then_inc(xdtd_ready, 1)
                    pool.wait_ge(cdk_ready, gi + 1)
                    pool.tensor_tensor(out=AB[:, :, META:T], in0=AB[:, :, META:T],
                                       in1=xc[:, ZT + SG + g, META:T].unsqueeze(1).to_broadcast([P, HG, T - META]),
                                       op=ALU.mult).then_inc(cdec_ready, 1)
            summed(pool, 4)
            pool.dma_start(wr, router[0].rearrange("(k p) e -> p k e", p=P)).then_inc(inputs_in[12], 16)
            pool.wait_ge(inputs_in[12], 16)

        @block.vector
        def _(dve):
            steps = [0]

            def link(ins):
                steps[0] += 1
                ins.then_inc(dve_step, 1)
                dve.wait_ge(dve_step, steps[0])

            def use(name, R=None, rdy=None):
                R = R or A
                assert R.who(name)[0] == "dve"
                dve.wait_ge(rdy or a_ready["dve"], R.who(name)[1])
                return ps[R.bank(name)]

            V = nc.vector
            dve.wait_ge(consts_done, 1)
            for t in range(KD):
                bk = use(("hin", t))
                V.tensor_copy(hT[:, t, :], bk[:, 0:T]).then_inc(a_taken["dve"], 1)
            V.tensor_copy(par, use(("par",))[:, 0:NPR]).then_inc(a_taken["dve"], 1)
            V.tensor_copy(cw.rearrange("p a b -> p (a b)"), use(("cw",))[:, 0:CK * DEPTH * XT])\
                .then_inc(a_taken["dve"], 1)
            bk = use(("dsk",))
            V.tensor_copy(dskc, bk[:, 0:DEPTH * ZT]).then_inc(a_taken["dve"], 1)
            dve.wait_ge(a_taken["dve"], A.who(("dsk",))[1])
            dve.wait_ge(a_exp, 1)
            link(V.tensor_scalar(acol[0:SH, :], acol[0:SH, :], -1.0, None, ALU.mult))

            def recip(name):
                emptied(dve, name)
                link(V.reciprocal(rs, rs))

            def scaled(dst, src, n, pc):
                for t in range(n):
                    last = V.scalar_tensor_tensor(out=dst[:, t, :], in0=src[:, t, :], scalar=par[:, pc + t:pc + t + 1],
                                                  in1=rs, op0=ALU.mult, op1=ALU.mult)
                last.then_inc(normed, 1)

            for li in range(DEPTH):
                recip(("ssq", li, 0))
                scaled(xn, hT, KD, PR_MIX + li * KD)
                xorder = [t - FT_X for c in IN_CHUNKS for t in in_tiles(*c) if FT_X <= t < FT_DT]

                def conv(m):
                    n_ = li * XT + m
                    ft = xorder[m]
                    r_ = raw[:, n_ % 2, :]
                    a_ = cacc[:, n_ % 2, :]
                    emptied(dve, ("proj", li, FT_X + ft))
                    if n_ >= 2:
                        dve.wait_ge(xc_ready, n_ - 1)
                    link(V.tensor_scalar(a_, r_[:, 0:T], cw[:, 0, li * XT + ft:li * XT + ft + 1], None, ALU.mult))
                    for w in range(1, CK):
                        ins = V.scalar_tensor_tensor(out=a_, in0=r_[:, w:w + T],
                                                     scalar=cw[:, w, li * XT + ft:li * XT + ft + 1],
                                                     in1=a_, op0=ALU.mult, op1=ALU.add)
                        if w < CK - 1:
                            link(ins)
                    ins.then_inc(conv_done, 1)

                def decay():
                    s24 = [d[0:SH, :] for d in dts]
                    dve.wait_ge(dt_act, 3 * li + 2)
                    V.tensor_scalar(s24[3], s24[2], 1.0, None, ALU.add).then_inc(dt_dve, 1)
                    dve.wait_ge(dt_dve, li + 1)
                    link(V.tensor_scalar(s24[5], s24[3], -1.0, None, ALU.add))
                    link(V.tensor_scalar(s24[1], s24[5], 0.0, None, ALU.is_equal))
                    link(V.tensor_tensor(out=s24[5], in0=s24[5], in1=s24[1], op=ALU.add))
                    link(V.reciprocal(s24[5], s24[5]))
                    link(V.tensor_tensor(out=s24[5], in0=s24[5], in1=s24[2], op=ALU.mult))
                    dve.wait_ge(dt_act, 3 * li + 3)
                    link(V.tensor_tensor(out=s24[4], in0=s24[4], in1=s24[1], op=ALU.add))
                    link(V.tensor_tensor(out=s24[5], in0=s24[5], in1=s24[4], op=ALU.mult))
                    link(V.scalar_tensor_tensor(out=s24[6], in0=s24[0], scalar=0.0, in1=s24[5], op0=ALU.max, op1=ALU.add))
                    link(V.tensor_scalar(s24[1], s24[6], acol[0:SH, li:li + 1], None, ALU.mult))
                    for c, (t0, L) in enumerate(CH):
                        last = V.tensor_tensor_scan(s24[7][:, t0:t0 + L], ones[0:SH, 0:L], s24[1][:, t0:t0 + L],
                                                    0.0, ALU.mult, ALU.add)
                    last.then_inc(acs_ready, 1)
                    bk = use(("small", li), B, b_ready)
                    V.tensor_copy(dtm[0:META, 0:2, :], bk[0:META, 0:2 * SH].rearrange("p (a b) -> p a b", a=2))
                    V.tensor_copy(dtm[:, 2:6, :], bk[:, 2 * SH:6 * SH].rearrange("p (a b) -> p a b", a=4))\
                        .then_inc(b_taken, 1)

                conv(0)
                conv(1)
                decay()
                for m in range(2, XT):
                    conv(m)
                dve.wait_ge(b_taken, B.who(("small", li))[1])
                dve.wait_ge(xc_ready, XT * (li + 1))
                def ssd_weights(g):
                    gi = li * SG + g
                    dve.wait_ge(acs_in, 16 * (gi + 1))
                    link(V.memset(Wt[:, :, 0:META], 0.0))
                    for h in range(HG):
                        for c, (t0, L) in enumerate(CH):
                            last = V.scalar_tensor_tensor(out=Wt[0:L, h, t0:t0 + L], in0=AB[0:L, h, t0:t0 + L],
                                                          scalar=dtm[0:L, 2 * c + 1, g * HG + h:g * HG + h + 1],
                                                          in1=mask_sl[0:L, 0:L], op0=ALU.subtract, op1=ALU.add)
                    last.then_inc(seg_ready, 1)
                    bk = use(("cbt", li, g), B, b_ready)
                    V.tensor_copy(cbt[0:META, 0:META], bk[0:META, 0:META])
                    V.tensor_copy(cbt[:, META:T], bk[:, META:T]).then_inc(b_taken, 1)
                    bk = use(("btm", li, g), B, b_ready)
                    V.tensor_copy(btm[0:META, 0, :], bk[0:META, 0:P])
                    V.tensor_copy(btm[:, 1, :], bk[:, P:2 * P]).then_inc(b_taken, 1)
                    for c, (t0, L) in enumerate(CH):
                        for r in range(2):
                            bk = use(("xa", li, g, c, r), B, b_ready)
                            hh = HG // 2
                            V.tensor_tensor(
                                out=xdt[0:L, c, r * GP // 2:(r + 1) * GP // 2].rearrange("p (h d) -> p h d", d=SP_),
                                in0=bk[0:L, 0:GP // 2].rearrange("p (h d) -> p h d", d=SP_),
                                in1=dtm[0:L, 2 * c, g * HG + r * hh:g * HG + (r + 1) * hh].unsqueeze(2)
                                .to_broadcast([L, hh, SP_]), op=ALU.mult).then_inc(b_taken, 1)
                    dve.wait_ge(b_taken, B.who(("xa", li, g, NC - 1, 1))[1])
                    dve.wait_ge(dec_ready, gi + 1)
                    V.tensor_copy(dl[0:META, 0, :], Wt[0:META, :, META - 1])
                    V.tensor_copy(dl[:, 1, :], Wt[:, :, META + P - 1]).then_inc(last_dec, 1)
                    dve.wait_ge(last_dec, gi + 1)
                    V.tensor_tensor(out=Wt, in0=Wt, in1=cbt.unsqueeze(1).to_broadcast([P, HG, T]), op=ALU.mult)\
                        .then_inc(wt_ready, 1)
                    dve.wait_ge(ab_exp, gi + 1)
                    V.tensor_copy(cdk, AB[:, :, META + P - 1]).then_inc(cdk_ready, 1)
                    dve.wait_ge(cdk_ready, gi + 1)

                def ssd_finish(g):
                    gi = li * SG + g
                    for r in range(2):
                        bk = use(("st", li, g, 0, r), B, b_ready)
                        V.tensor_copy(hst[:, 0, r * GP // 2:(r + 1) * GP // 2], bk[:, 0:GP // 2]).then_inc(b_taken, 1)
                    dve.wait_ge(b_taken, B.who(("st", li, g, 0, 1))[1])
                    link(V.tensor_tensor(out=hst[:, 1, :].rearrange("p (h d) -> p h d", d=SP_),
                                         in0=hst[:, 0, :].rearrange("p (h d) -> p h d", d=SP_),
                                         in1=cdk[:, :].unsqueeze(2).to_broadcast([P, HG, SP_]), op=ALU.mult))
                    for r in range(2):
                        bk = use(("st", li, g, 1, r), B, b_ready)
                        hh = hst[:, 1, r * GP // 2:(r + 1) * GP // 2]
                        V.tensor_tensor(out=hh, in0=hh, in1=bk[:, 0:GP // 2], op=ALU.add).then_inc(b_taken, 1)
                    for j in range(GT):
                        bk, t = use(("y", li, g, j)), GT * g + j
                        emptied(dve, ("proj", li, FT_Z + t))
                        if j >= 2:
                            dve.wait_ge(gated, SG * GT * li + t - 1)
                        V.scalar_tensor_tensor(out=cacc[:, t % 2, :], in0=xc[:, t, :],
                                               scalar=dskc[:, DEPTH * t + li:DEPTH * t + li + 1], in1=bk[:, 0:T],
                                               op0=ALU.mult, op1=ALU.add).then_inc(a_taken["dve"], 1)
                        emptied(dve, ("y", li, g, j))
                        V.tensor_tensor(out=mixT[:, QT + t, :], in0=cacc[:, t % 2, :], in1=mixT[:, QT + t, :], op=ALU.mult)\
                            .then_inc(gated, 1)

                ssd_weights(0)
                ssd_finish(0)
                ssd_weights(1)

                def scale_scores(h):
                    bk = use(("score", li, h))
                    if h >= 2:
                        dve.wait_ge(a_ready["act"], A.who(("pt2", li, h - 2))[1])
                    masks = (mask1[0:META, META:2 * META], mask1, mask2)
                    for c, (at, keys) in enumerate(((0, META), (META, META + P), (2 * META + P, T))):
                        L = CH[c][1]
                        last = V.scalar_tensor_tensor(out=S[0:L, h % 2, at:at + keys], in0=bk[0:L, at:at + keys],
                                                      scalar=HD ** -0.5, in1=masks[c], op0=ALU.mult, op1=ALU.add)
                    last.then_inc(a_taken["dve"], 1)
                    emptied(dve, ("score", li, h))
                    for c, (at, keys) in enumerate(((0, META), (META, META + P), (2 * META + P, T))):
                        L = CH[c][1]
                        last = V.tensor_reduce(smax[0:L, h, c:c + 1], S[0:L, h % 2, at:at + keys], AX.X, ALU.max)
                    link(last)
                    V.tensor_scalar(snm[:, h, :], smax[:, h, :], sinkb[:, li * HEADS + h:li * HEADS + h + 1], -1.0,
                                    ALU.max, ALU.mult).then_inc(sc_ready, 1)

                def norm_scores(h):
                    dve.wait_ge(pexp, HEADS * li + h + 1)
                    link(V.tensor_tensor(out=srec[:, h, :], in0=ssum[:, h, :], in1=ssink[:, h, :], op=ALU.add))
                    link(V.reciprocal(srec[:, h, :], srec[:, h, :]))
                    for c, (at, keys) in enumerate(((0, META), (META, META + P), (2 * META + P, T))):
                        L = CH[c][1]
                        last = V.tensor_scalar(S[0:L, h % 2, at:at + keys], S[0:L, h % 2, at:at + keys],
                                               srec[0:L, h, c:c + 1], None, ALU.mult)
                    last.then_inc(p_ready, 1)

                dve.wait_ge(inputs_in[13], 16)
                for h in range(HEADS):
                    scale_scores(h)
                    if h:
                        norm_scores(h - 1)
                norm_scores(HEADS - 1)
                ssd_finish(1)
                for s, (t0, n, pc) in enumerate(((QT, GT, PR_SSM + li * ZT), (QT + GT, GT, PR_SSM + li * ZT + GT),
                                                 (0, QT, PR_ATT + li * QT))):
                    recip(("ssqy", li, s))
                    scaled(mixT[:, t0:t0 + n, :], mixT[:, t0:t0 + n, :], n, pc)

                def add_residual(name, t):
                    bk = use(name)
                    V.tensor_tensor(out=hT[:, t, :], in0=hT[:, t, :], in1=bk[:, 0:T], op=ALU.add)\
                        .then_inc(a_taken["dve"], 1)

                for t in range(KD):
                    add_residual(("out", li, t), t)
                recip(("ssq", li, 1))
                scaled(xn, hT, KD, PR_FFN + li * KD)
                if li == 0:
                    for f in range(FT):
                        bk = use(("u", f))
                        emptied(dve, ("g", f))
                        V.tensor_tensor(out=hf[:, f, :], in0=cacc[:, f % 2, :], in1=bk[:, 0:T], op=ALU.mult)\
                            .then_inc(a_taken["dve"], 1)
                    for t in range(KD):
                        add_residual(("down", t), t)
            lg, mk, ea = [tiles(rt[:, o:o + 2 * NE], 2) for o in (0, 32, 48)]
            mx, sume = rt[:, 16:18], rt[:, 18:20]
            big, big2 = [rt[:, o:o + 2 * NE * NE].rearrange("p (c e j) -> p c e j", c=2, e=NE) for o in (64, 192)]
            full = [P, 2, NE, NE]
            V.tensor_copy(lg, use(("logit",))[:, 0:2 * NE].rearrange("p (c e) -> p c e", c=2)).then_inc(a_taken["dve"], 1)
            emptied(dve, ("logit",))
            own, oth = lg.unsqueeze(3).to_broadcast(full), lg.unsqueeze(2).to_broadcast(full)
            V.tensor_tensor(out=big, in0=own, in1=oth, op=ALU.is_lt)
            V.tensor_reduce(mx, lg, AX.X, ALU.max)
            link(V.tensor_tensor(out=big2, in0=own, in1=oth, op=ALU.is_equal))
            link(V.tensor_tensor(out=big2, in0=big2, in1=tri8.unsqueeze(1).to_broadcast(full), op=ALU.mult))
            link(V.tensor_tensor(out=big, in0=big, in1=big2, op=ALU.add))
            link(V.tensor_reduce(mk, big, AX.X, ALU.add))
            V.tensor_scalar(mk, mk, 1.5, None, ALU.is_lt).then_inc(mask_ready, 1)
            V.tensor_tensor(out=ea, in0=lg, in1=mx.unsqueeze(2).to_broadcast([P, 2, NE]), op=ALU.subtract)\
                .then_inc(mask_ready, 1)
            dve.wait_ge(route_exp, 1)
            link(V.tensor_tensor(out=ea, in0=ea, in1=mk, op=ALU.mult))
            link(V.tensor_reduce(sume, ea, AX.X, ALU.add))
            link(V.reciprocal(sume, sume))
            for b in range(2):
                V.tensor_tensor(out=cb[:, :, b * NE:(b + 1) * NE], in0=ea, in1=sume.unsqueeze(2).to_broadcast([P, 2, NE]),
                                op=ALU.mult)
            bk = use(("pos",))
            link(V.scalar_tensor_tensor(out=px[:, :, 0:NE], in0=bk[:, 0:2 * NE].rearrange("p (c e) -> p c e", c=2),
                                        scalar=1.0, in1=mk, op0=ALU.add, op1=ALU.mult))
            link(V.tensor_scalar(px[:, :, 0:NE], px[:, :, 0:NE], -1.0, None, ALU.add))
            link(V.tensor_scalar(px[:, :, NE:2 * NE], px[:, :, 0:NE], -float(P), None, ALU.add))
            over, incl, rk = [rt[0:1, o:o + NE] for o in (64, 72, 80)]
            lst = rt[0:1, 96:96 + 25]
            link(V.memset(lst, 0.0))
            V.tensor_copy(lst[:, 0:NE], slots_row[0:1, 0:NE])
            V.tensor_copy(lst[:, MAXI:MAXI + NE], slots_row[0:1, 0:NE])
            V.tensor_scalar(over, bk[0:1, 2 * NE:3 * NE], P + 0.5, None, ALU.is_gt).then_inc(a_taken["dve"], 1)
            emptied(dve, ("pos",))
            link(V.tensor_tensor_scan(incl, ones[0:1, 0:NE], over, 0.0, ALU.mult, ALU.add))
            link(V.tensor_tensor(out=rk, in0=incl, in1=over, op=ALU.subtract))
            link(V.tensor_scalar(lst[:, 24:25], incl[:, NE - 1:NE], float(NE), None, ALU.add))
            for j in range(MAXI - 1 - NE):
                t = rt[0:1, 128 + 8 * j:136 + 8 * j]
                link(V.scalar_tensor_tensor(out=t, in0=rk, scalar=float(j), in1=over, op0=ALU.is_equal, op1=ALU.mult))
                link(V.tensor_tensor(out=t, in0=t, in1=slots_row[0:1, 0:NE], op=ALU.mult))
                link(V.tensor_reduce(lst[:, MAXI + NE + j:MAXI + NE + j + 1], t, AX.X, ALU.add))
            link(V.tensor_scalar(lst[:, NE:MAXI - 1], lst[:, MAXI + NE:2 * MAXI - 1], float(NE), None, ALU.add))
            V.tensor_copy(rt[0:1, 340:365].bitcast(I32), lst).then_inc(list_ready, 1)
            dve.sem_inc(h_made, 2)
            dve.sem_inc(scat_taken, 4)
            dve.sem_inc(ht_low, 1)
            dve.wait_ge(list_ready, 1)
            n_items = dve.value_load(rt[0:1, 364:365].bitcast(I32), min_val=NE, max_val=MAXI - 1)
            emptied(dve, ("htm", 1, 1))
            with dve.Fori(0, n_items) as i:
                code = dve.value_load(rt[0:1, 340:352].bitcast(I32)[:, bass.ds(i, 1)], min_val=0, max_val=2 * NE - 1)
                for c in range(2):
                    V.tensor_scalar(sel[:, c, :], slots_row, px[:, c, bass.ds(code, 1)], None, ALU.is_equal)
                    last = V.tensor_scalar(selg[:, c, :], slots_row, px[:, c, bass.ds(code, 1)],
                                           cb[:, c, bass.ds(code, 1)], ALU.is_equal, ALU.mult)
                last.then_inc(sel_ready, 1)

                def low(kind, c):
                    dve.wait_ge(hi_ready[kind], i * EN + (c + 1))
                    V.tensor_tensor(out=wlo[kind][:, c % 2, :], in0=raw_w[kind][:, c % 2, :],
                                    in1=whi[kind][:, c % 2, :].bitcast(F32), op=ALU.subtract).then_inc(lo_ready[kind], 1)

                def low_h(c):
                    dve.wait_ge(ht_taken, i * EN + (c + 1))
                    V.tensor_tensor(out=hlo[:, c % 2, :], in0=ps[4][:, 0:EC], in1=hhi[:, c % 2, :].bitcast(F32),
                                    op=ALU.subtract).then_inc(ht_low, 1)

                def gate(c):
                    dve.wait_ge(g_silu, i * EN + (c + 3))
                    dve.wait_ge(u_done, i * EN + (c + 3))
                    V.tensor_tensor(out=hs[:, c % 2, :], in0=hs[:, c % 2, :], in1=ps[2 * (c % 2) + 1][:, 0:EC],
                                    op=ALU.mult).then_inc(h_made, 1)

                low(0, 0)
                for r in range(2):
                    dve.wait_ge(xg_ready, i * 2 + (r + 1))
                    V.tensor_tensor(out=xlo[:, 4 * r:4 * r + 4, :],
                                    in0=ps[(7, 4)[r]][:, :].rearrange("p (a b) -> p a b", a=4),
                                    in1=xhi[:, 4 * r:4 * r + 4, :].bitcast(F32), op=ALU.subtract).then_inc(xlo_ready, 1)
                low(1, 0)
                for c in range(EN):
                    if c:
                        low_h(c - 1)
                    gate(c)
                    if c + 1 < EN:
                        low(0, c + 1)
                        low(1, c + 1)
                    low(2, c)
                low_h(EN - 1)
                for n in range(4):
                    dve.wait_ge(scat_done, i * 4 + (n + 1))
                    a_ = acc[:, n // 2, (n % 2) * WC:(n % 2 + 1) * WC]
                    V.tensor_tensor(out=a_, in0=a_, in1=ps[n][:, :], op=ALU.add).then_inc(scat_taken, 1)
            dve.wait_ge(fin_root, 3)
            link(V.reciprocal(fin[:, 4:6], fin[:, 2:4]))
            dve.wait_ge(inputs_in[14], 16)
            for c in range(2):
                V.scalar_tensor_tensor(out=acc[:, c, :], in0=acc[:, c, :], scalar=fin[:, 4 + c:5 + c], in1=gfin,
                                       op0=ALU.mult, op1=ALU.mult).then_inc(out_ready, 1)


_INS = ["x", "meta_tokens", "norm_mix", "w_in", "conv_w", "conv_b", "dt_bias", "a_log", "d_skip", "ssm_norm",
        "attn_norm", "sinks", "w_out", "norm_ffn", "ffn_w1", "ffn_w3", "ffn_w2", "router", "moe_w1", "moe_w3",
        "moe_w2", "final_norm"]


def kernel(**inputs):
    import numpy as _np
    import concourse.bacc as _bacc
    from concourse.bass_utils import run_bass_kernel_spmd as _run

    nc = _bacc.Bacc("TRN2", target_bir_lowering=False, num_devices=1)
    arrays, args = {}, []
    for name in _INS:
        a = _np.ascontiguousarray(inputs[name])
        arrays[f"in_{name}"] = a
        args.append(nc.dram_tensor(f"in_{name}", a.shape, F32, kind="ExternalInput").ap())
    args.append(nc.dram_tensor("out_0", (1, SEQ, D), F32, kind="ExternalOutput").ap())
    trunk(nc, *args)
    r = _run(nc, [arrays], core_ids=[0])
    return r.results[0]["out_0"]
```
